# Optimizing a Trainium2 kernel written in Bass

```python
import math
import jax
import jax.numpy as jnp
from jax import lax
import numpy as np

D_MODEL = 1024
BATCH = 1
SEQ = 1024
DEPTH = 2

N_META = 16
HEAD_DIM = 128
HA = 4
HB = 4
DA = HA * HEAD_DIM
DB = HB * HEAD_DIM
CONV_WIDTH = 4
CHUNK = 64
Q_BLOCK = 128
W_IN_COLS = 4 * DA + 2 * HA + 3 * DB
SSM_WIDTH = D_MODEL
GROUP = 16
N_GROUPS = SSM_WIDTH // GROUP
STATE = 64
D_FF = int(math.ceil(8 * D_MODEL / 3 / 256)) * 256
N_EVEN = (DEPTH + 1) // 2
N_ODD = DEPTH // 2
EPS = 1e-6

kernel_name = "hybrid_deltanet_stickbreak_s5_trunk"

def rms_norm(x, w):
    xf = x.astype(jnp.float32)
    y = xf * lax.rsqrt(jnp.mean(xf * xf, axis=-1, keepdims=True) + EPS)
    return (y * w.astype(jnp.float32)).astype(x.dtype)

def gated_rms_norm(o, z, w):
    of = o.astype(jnp.float32)
    y = of * lax.rsqrt(jnp.mean(of * of, axis=-1, keepdims=True) + EPS) * w.astype(jnp.float32)
    return (y * jax.nn.silu(z.astype(jnp.float32))).astype(z.dtype)

def l2_normalize(t):
    return t * lax.rsqrt(jnp.sum(t * t, axis=-1, keepdims=True) + EPS)

def pad_seq(t, front, back):
    return jnp.pad(t, [(0, 0), (front, back)] + [(0, 0)] * (t.ndim - 2))

def causal_depthwise_conv(x, w):
    k_len = w.shape[0]
    return lax.conv_general_dilated(
        x, w[:, None, :], window_strides=(1,), padding=[(k_len - 1, 0)],
        dimension_numbers=("NWC", "WIO", "NWC"), feature_group_count=x.shape[-1])

def gated_delta_rule_chunked(q, k, v, g, beta):
    bsz, seq_len, n_h, dk = q.shape
    dv = v.shape[-1]
    n_chunks = seq_len // CHUNK

    def chunks(t):
        t = t.reshape((bsz, n_chunks, CHUNK, n_h) + t.shape[3:])
        return jnp.moveaxis(jnp.moveaxis(t, 1, 0), 3, 2)

    qc, kc, vc, gc, bc = chunks(q), chunks(k), chunks(v), chunks(g), chunks(beta)
    G = jnp.cumsum(gc, axis=-1)
    incl = jnp.tril(jnp.ones((CHUNK, CHUNK), dtype=bool))
    strict = jnp.tril(jnp.ones((CHUNK, CHUNK), dtype=bool), -1)
    diff = G[..., :, None] - G[..., None, :]
    decay = jnp.where(incl, jnp.exp(jnp.where(incl, diff, 0.0)), 0.0)
    kb = kc * bc[..., None]
    lower = jnp.where(strict, jnp.einsum("nbhid,nbhjd->nbhij", kb, kc) * decay, 0.0)
    eye = jnp.eye(CHUNK, dtype=lower.dtype)
    rhs = jnp.concatenate([vc * bc[..., None], kb * jnp.exp(G)[..., None]], axis=-1)
    sol = lax.linalg.triangular_solve(lower + eye, rhs, left_side=True, lower=True,
                                      unit_diagonal=True)
    u_c, w_c = sol[..., :dv], sol[..., dv:]
    qk = jnp.where(incl, jnp.einsum("nbhid,nbhjd->nbhij", qc, kc) * decay, 0.0)
    q_dec = qc * jnp.exp(G)[..., None]
    k_dec = kc * jnp.exp(G[..., -1:] - G)[..., None]
    g_last = jnp.exp(G[..., -1])

    def step(S, xs):
        qk_n, qd_n, kd_n, u_n, w_n, gl_n = xs
        v_new = u_n - jnp.einsum("bhck,bhkv->bhcv", w_n, S)
        o = jnp.einsum("bhck,bhkv->bhcv", qd_n, S) + jnp.einsum("bhij,bhjv->bhiv", qk_n, v_new)
        S = S * gl_n[..., None, None] + jnp.einsum("bhck,bhcv->bhkv", kd_n, v_new)
        return S, o

    S0 = jnp.zeros((bsz, n_h, dk, dv), dtype=qc.dtype)
    _, o = lax.scan(step, S0, (qk, q_dec, k_dec, u_c, w_c, g_last))
    o = jnp.moveaxis(jnp.moveaxis(o, 2, 3), 0, 1)
    return o.reshape(bsz, seq_len, n_h, dv)

def stick_breaking_attention(q, k, v):
    bsz, seq_len, n_h, dh = q.shape
    n_blocks = -(-seq_len // Q_BLOCK)
    lp = n_blocks * Q_BLOCK
    q, k, v = pad_seq(q, 0, lp - seq_len), pad_seq(k, 0, lp - seq_len), pad_seq(v, 0, lp - seq_len)
    scale = dh ** -0.5
    key_pos = jnp.arange(lp)

    def block(start):
        qb = lax.dynamic_slice_in_dim(q, start, Q_BLOCK, axis=1)
        z = jnp.einsum("bqhd,bkhd->bhqk", qb, k, preferred_element_type=jnp.float32) * scale
        causal = key_pos[None, :] < (start + jnp.arange(Q_BLOCK))[:, None]
        log_1m = jnp.where(causal, jax.nn.log_sigmoid(-z), 0.0)
        csum = jnp.cumsum(log_1m, axis=-1)
        log_w = jax.nn.log_sigmoid(z) + (csum[..., -1:] - csum)
        w = jnp.where(causal, jnp.exp(log_w), 0.0)
        return jnp.einsum("bhqk,bkhd->bqhd", w.astype(v.dtype), v)

    out = lax.map(block, jnp.arange(n_blocks) * Q_BLOCK)
    out = jnp.moveaxis(out, 0, 1).reshape(bsz, lp, n_h, dh)
    return out[:, :seq_len]

def deltanet_stickbreak_mixer(u, w_in, conv_w, a_log, dt_bias, out_norm, w_out):
    bsz, seq_len, _ = u.shape
    proj = u @ w_in
    qkv_a, z_a, b_a, a_a, qkv_b = jnp.split(
        proj, [3 * DA, 4 * DA, 4 * DA + HA, 4 * DA + 2 * HA], axis=-1)
    qkv_a = jax.nn.silu(causal_depthwise_conv(qkv_a, conv_w)).astype(jnp.float32)
    q_a, k_a, v_a = (t.reshape(bsz, seq_len, HA, HEAD_DIM) for t in jnp.split(qkv_a, 3, axis=-1))
    q_a = l2_normalize(q_a) * HEAD_DIM ** -0.5
    k_a = l2_normalize(k_a)
    beta = jax.nn.sigmoid(b_a.astype(jnp.float32))
    g = -jnp.exp(a_log.astype(jnp.float32)) * jax.nn.softplus(
        a_a.astype(jnp.float32) + dt_bias.astype(jnp.float32))
    front = CHUNK - N_META
    back = (-(seq_len + front)) % CHUNK
    o_a = gated_delta_rule_chunked(pad_seq(q_a, front, back), pad_seq(k_a, front, back),
                                   pad_seq(v_a, front, back), pad_seq(g, front, back),
                                   pad_seq(beta, front, back))[:, front:front + seq_len]
    o_a = gated_rms_norm(o_a, z_a.reshape(bsz, seq_len, HA, HEAD_DIM), out_norm)
    q_b, k_b, v_b = (t.reshape(bsz, seq_len, HB, HEAD_DIM) for t in jnp.split(qkv_b, 3, axis=-1))
    o_b = stick_breaking_attention(q_b, k_b, v_b)
    o = jnp.concatenate([o_a.reshape(bsz, seq_len, DA), o_b.reshape(bsz, seq_len, DB)], axis=-1)
    return o @ w_out

def s5_mixer(u, w_in, lam_re, lam_im, log_step, b_re, b_im, c_re, c_im, d_skip, w_glu):
    bsz, seq_len, _ = u.shape
    h = (u @ w_in).astype(jnp.float32)
    hg = h.reshape(bsz, seq_len, N_GROUPS, GROUP)
    lam_re = lam_re.astype(jnp.float32)
    lam_im = lam_im.astype(jnp.float32)
    dt = jnp.exp(log_step.astype(jnp.float32))[:, None]
    mag = jnp.exp(lam_re * dt)
    a_re = mag * jnp.cos(lam_im * dt)
    a_im = mag * jnp.sin(lam_im * dt)
    den = lam_re * lam_re + lam_im * lam_im
    f_re = ((a_re - 1.0) * lam_re + a_im * lam_im) / den
    f_im = (a_im * lam_re - (a_re - 1.0) * lam_im) / den
    b_re = b_re.astype(jnp.float32)
    b_im = b_im.astype(jnp.float32)
    bb_re = f_re[..., None] * b_re - f_im[..., None] * b_im
    bb_im = f_re[..., None] * b_im + f_im[..., None] * b_re
    bu_re = jnp.einsum("gpc,blgc->lbgp", bb_re, hg)
    bu_im = jnp.einsum("gpc,blgc->lbgp", bb_im, hg)
    a_re_l = jnp.broadcast_to(a_re, (seq_len, 1, N_GROUPS, STATE))
    a_im_l = jnp.broadcast_to(a_im, (seq_len, 1, N_GROUPS, STATE))

    def combine(e1, e2):
        ar1, ai1, br1, bi1 = e1
        ar2, ai2, br2, bi2 = e2
        return (ar1 * ar2 - ai1 * ai2, ar1 * ai2 + ai1 * ar2,
                ar2 * br1 - ai2 * bi1 + br2, ar2 * bi1 + ai2 * br1 + bi2)

    _, _, x_re, x_im = lax.associative_scan(combine, (a_re_l, a_im_l, bu_re, bu_im), axis=0)
    y = (jnp.einsum("gcp,lbgp->blgc", c_re.astype(jnp.float32), x_re)
         - jnp.einsum("gcp,lbgp->blgc", c_im.astype(jnp.float32), x_im))
    y = y.reshape(bsz, seq_len, SSM_WIDTH) + d_skip.astype(jnp.float32) * h
    y = jax.nn.gelu(y).astype(u.dtype)
    val, gate = jnp.split(y @ w_glu, 2, axis=-1)
    return val * jax.nn.sigmoid(gate)

def swiglu_ffn(x, w_gate, w_up, w_down):
    return (jax.nn.silu(x @ w_gate) * (x @ w_up)) @ w_down

def setup_inputs(seed: int = 0) -> dict:
    key = jax.random.key(seed)
    ks = jax.random.split(key, 32)
    f32 = jnp.float32

    def nrm(k, shape, scale):
        return jax.random.normal(k, shape, f32) * scale

    def gain(k, shape):
        return 1.0 + 0.02 * jax.random.normal(k, shape, f32)

    dt = jnp.exp(jax.random.uniform(ks[13], (N_EVEN, HA), f32, math.log(1e-3), math.log(1e-1)))
    lam_im0 = jnp.pi * jnp.arange(STATE, dtype=f32)
    return {
        "x": nrm(ks[0], (BATCH, SEQ, D_MODEL), 1.0),
        "meta_tokens": nrm(ks[1], (N_META, D_MODEL), 1.0),
        "norm_mix_pre": gain(ks[2], (DEPTH, D_MODEL)),
        "norm_mix_post": gain(ks[3], (DEPTH, D_MODEL)),
        "norm_ffn_pre": gain(ks[4], (DEPTH, D_MODEL)),
        "norm_ffn_post": gain(ks[5], (DEPTH, D_MODEL)),
        "ffn_w_gate": nrm(ks[6], (DEPTH, D_MODEL, D_FF), D_MODEL ** -0.5),
        "ffn_w_up": nrm(ks[7], (DEPTH, D_MODEL, D_FF), D_MODEL ** -0.5),
        "ffn_w_down": nrm(ks[8], (DEPTH, D_FF, D_MODEL), D_FF ** -0.5),
        "hyb_w_in": nrm(ks[9], (N_EVEN, D_MODEL, W_IN_COLS), D_MODEL ** -0.5),
        "hyb_conv_w": nrm(ks[10], (N_EVEN, CONV_WIDTH, 3 * DA), CONV_WIDTH ** -0.5),
        "dn_a_log": jnp.log(jax.random.uniform(ks[11], (N_EVEN, HA), f32, 1.0, 16.0)),
        "dn_dt_bias": dt + jnp.log(-jnp.expm1(-dt)),
        "dn_out_norm": gain(ks[12], (N_EVEN, HEAD_DIM)),
        "hyb_w_out": nrm(ks[14], (N_EVEN, DA + DB, D_MODEL), (DA + DB) ** -0.5),
        "ssm_w_in": nrm(ks[15], (N_ODD, D_MODEL, SSM_WIDTH), D_MODEL ** -0.5),
        "ssm_lambda_re": -0.5 + 0.01 * jax.random.normal(ks[16], (N_ODD, N_GROUPS, STATE), f32),
        "ssm_lambda_im": lam_im0 + 0.01 * jax.random.normal(ks[17], (N_ODD, N_GROUPS, STATE), f32),
        "ssm_log_step": jax.random.uniform(ks[18], (N_ODD, N_GROUPS), f32, math.log(1e-3), math.log(1e-1)),
        "ssm_b_re": nrm(ks[19], (N_ODD, N_GROUPS, STATE, GROUP), (2 * GROUP) ** -0.5),
        "ssm_b_im": nrm(ks[20], (N_ODD, N_GROUPS, STATE, GROUP), (2 * GROUP) ** -0.5),
        "ssm_c_re": nrm(ks[21], (N_ODD, N_GROUPS, GROUP, STATE), (2 * STATE) ** -0.5),
        "ssm_c_im": nrm(ks[22], (N_ODD, N_GROUPS, GROUP, STATE), (2 * STATE) ** -0.5),
        "ssm_d": nrm(ks[23], (N_ODD, SSM_WIDTH), 1.0),
        "ssm_w_glu": nrm(ks[24], (N_ODD, SSM_WIDTH, 2 * D_MODEL), SSM_WIDTH ** -0.5),
    }

def reference(x, meta_tokens, norm_mix_pre, norm_mix_post, norm_ffn_pre, norm_ffn_post,
              ffn_w_gate, ffn_w_up, ffn_w_down, hyb_w_in, hyb_conv_w, dn_a_log, dn_dt_bias,
              dn_out_norm, hyb_w_out, ssm_w_in, ssm_lambda_re, ssm_lambda_im, ssm_log_step,
              ssm_b_re, ssm_b_im, ssm_c_re, ssm_c_im, ssm_d, ssm_w_glu):
    bsz = x.shape[0]
    meta = jnp.broadcast_to(meta_tokens[None].astype(x.dtype), (bsz, N_META, x.shape[-1]))
    h = jnp.concatenate([meta, x], axis=1)
    for i in range(DEPTH):
        j = i // 2
        hn = rms_norm(h, norm_mix_pre[i])
        if i % 2 == 0:
            m = deltanet_stickbreak_mixer(hn, hyb_w_in[j], hyb_conv_w[j], dn_a_log[j],
                                          dn_dt_bias[j], dn_out_norm[j], hyb_w_out[j])
        else:
            m = s5_mixer(hn, ssm_w_in[j], ssm_lambda_re[j], ssm_lambda_im[j], ssm_log_step[j],
                         ssm_b_re[j], ssm_b_im[j], ssm_c_re[j], ssm_c_im[j], ssm_d[j], ssm_w_glu[j])
        h = h + rms_norm(m.astype(h.dtype), norm_mix_post[i])
        hn = rms_norm(h, norm_ffn_pre[i])
        f = swiglu_ffn(hn, ffn_w_gate[i], ffn_w_up[i], ffn_w_down[i])
        h = h + rms_norm(f, norm_ffn_post[i])
    return h[:, N_META:]


_drawn_inputs = setup_inputs


def setup_inputs(seed=0):
    import zlib

    import numpy as np

    out = dict(_drawn_inputs(seed))
    spreads = {}
    factors = {'norm_mix_post': 2.724,
     'norm_ffn_post': 3.451,
     'dn_out_norm': 5.081,
     'ssm_lambda_re': 200.0,
     'ssm_lambda_im': 30.296,
     'ssm_log_step': 33.28,
     'ssm_b_re': 41.288,
     'ssm_b_im': 41.872,
     'ssm_c_re': 41.576,
     'ssm_c_im': 41.632}
    for name, (base, spread) in spreads.items():
        noise = np.random.default_rng([zlib.crc32(name.encode()), seed]).standard_normal(out[name].shape)
        drawn = base * np.exp(spread * noise) if base else spread * noise
        out[name] = jnp.asarray(drawn.astype(out[name].dtype))
    for name, factor in factors.items():
        out[name] = (out[name] * factor).astype(out[name].dtype)
    return out
```

```python
from contextlib import ExitStack

import numpy as np

import concourse.bass as bass
from concourse import mybir

F32 = mybir.dt.float32
F32R = mybir.dt.float32r
I32 = mybir.dt.int32
ALU = mybir.AluOpType
ACT = mybir.ActivationFunctionType

P = 128
N_META, SEQ, D = 16, 1024, 1024
T = N_META + SEQ
KT = D // P
HEADS = 4
HD = 128
EPS = 1e-6
D_FF = 2816
PAIRS = D_FF // (2 * P)

CUTS = [(0, 352), (352, 344), (696, 344)]
HALF_CUTS = [(0, 176), (176, 176), (352, 172), (524, 172), (696, 172), (868, 172)]
CW = 352

BLOCKS = (T + P - 1) // P
TAIL = T - (BLOCKS - 1) * P
T_ROWS = BLOCKS * P
T_PAD = (BLOCKS + 1) * P

DQ, DK, DV, DZ, SQ, SK, SV = 0, 4, 8, 12, 16, 20, 24
N_PROJ = 28

G_CH, STATE, CH = 16, 64, 8
N_GROUPS = D // G_CH
S_PAIRS = N_GROUPS // 2
NJ = T // CH
QP = 4
GPT = 8

SLOTS = 6
STREAM = [
    ("gates", 1, [5]),
    ("in_proj", 7, [0, 1, 2, 3]),
    ("w_out", 2, [0, 1, 2, 3]),
    ("ffn0", PAIRS, [0, 1, 2, 3, 4, 5]),
    ("ssm_in", 2, [0, 1, 2, 3]),
    ("glu", 4, [0, 1, 2, 3]),
    ("ffn1", PAIRS, [0, 1, 2, 3, 4, 5]),
]
N_SLABS = sum(n * len(s) for _, n, s in STREAM)

(MIX_PRE, MIX_POST, FFN_PRE, FFN_POST), W_CONV, W_ONORM, A_LOG, DT_BIAS, D_SKIP = (
    [0, 16, 32, 48], 64, 112, 113, 114, 115)
N_SMALL = 123
C_ID, C_ONES, C_INCL, C_STRICT, C_SHIFT, C_LEVEL, C_SEL = [P * i for i in (0, 1, 2, 3, 4, 6, 13)]
N_CONST = P * 21
LEVELS = 7
S_LRE, S_LIM, S_LOG, S_BRE, S_BIM, S_CRE, S_CIM = 0, 32, 64, 96, 608, 1120, 1632
N_S5 = 2144

TWO_PI_A = 6.28125
TWO_PI_B = float(np.float32(0.00193500518798828125))
TWO_PI_C = float(2 * np.pi - TWO_PI_A - TWO_PI_B)


GROUPS_BEFORE = {"gates": 0, "in_proj": 6, "w_out": 90, "ssm_in": 114, "glu": 138}
WT_BEFORE = [sum((i + 4) // 4 for i in range(b)) for b in range(BLOCKS)]
WT_GROUPS = 3 + sum((i + 4) // 4 for i in range(BLOCKS))
GATE_DVE = 3
S5_MARKS = 35


NORM_ORDER = ((0, 0), (1, 0), (0, 1), (2, 0), (1, 1), (2, 1))


def norm_steps(r):
    return [(c, m) for c, m in NORM_ORDER if (r > 0 or m == 1) and (r < 4 or m == 0)]


def norm_event(r, c, m):
    if r == 0:
        return c
    return 3 + 6 * (r - 1) + (NORM_ORDER.index((c, m)) if r < 4 else c)


class Chain:

    def __init__(self, eng, sem):
        self.eng, self.sem, self.n, self.loop = eng, sem, 0, None

    def __call__(self, ins):
        ins.then_inc(self.sem, 1)
        self.n += 1
        return ins

    def sync(self):
        if self.loop is None:
            self.eng.wait_ge(self.sem, self.n)
        else:
            i, per = self.loop
            self.eng.wait_ge(self.sem, i * per + self.n)

    def enter(self, i, i0, per):
        self.loop, self.start = (i, per), self.n
        self.n -= i0 * per
        self.i0 = i0

    def leave(self, count):
        i, per = self.loop
        assert self.n + self.i0 * per - self.start == per, (self.n + self.i0 * per - self.start, per)
        self.loop, self.n = None, self.start + count * per


def norm_views(carve, at):
    return {"h": [carve(at + KT * CW * i, KT, CW) for i in range(2)], "nb": carve(at + 2 * KT * CW, KT, CW),
            "sq": carve(at + 3 * KT * CW, KT // 2, CW),
            "rs": [carve(at + 7 * KT * CW // 2 + CW * i, CW) for i in range(2)]}


def conv_views(carve):
    at = 4 * T_ROWS
    return ([carve(at + (T + 4) * i, T + 3) for i in range(2)],
            [carve(at + 2 * (T + 4) + T * i, T) for i in range(2)],
            [carve(at + 2 * (T + 4) + T * (2 + i), T) for i in range(2)])


def ffn_views(carve):
    at = KT * T
    return [carve(at + CW * i, CW) for i in range(2)], [carve(at + CW * (2 + i), CW) for i in range(2)]


def dn_views(carve):
    v = {"rows": carve(0, T_ROWS), "cols": carve(T_ROWS, BLOCKS, 64), "state": carve(1728, 512)}
    for s in range(2):
        at = 2240 + 7700 * s
        v[s] = {x: carve(at + 512 * i, 512) for i, x in enumerate(
            ("q", "k", "v", "z", "kb", "qd", "eg", "lt", "qk", "x", "u", "t1", "t2", "vt", "kd"))}
        for i, x in enumerate(("ss", "ecol", "gl")):
            v[s][x] = carve(at + 512 * 15 + 4 * i, 4)
    return v


def sb_views(carve):
    v = {x: carve(T * i, T) for i, x in enumerate("qkv")}
    v["vt"], v["wt"] = carve(3 * T, BLOCKS * P), carve(3 * T + BLOCKS * P, BLOCKS, P)
    at = 3 * T + 2 * BLOCKS * P
    v["e"] = [carve(at + T * i, T) for i in range(3)]
    v["r"] = [carve(at + T * (3 + i), T) for i in range(2)]
    return v


def s5_views(carve):
    z, at = {}, 0

    def put(name, *shape, n=1):
        nonlocal at
        z[name] = [carve(at + i * int(np.prod(shape)), *shape) for i in range(n)]
        at += n * int(np.prod(shape))
        if n == 1:
            z[name] = z[name][0]
    put("ut", T, n=2)
    z["rot"] = [carve(QP * NJ * i, QP, NJ) for i in range(4)]
    put("par", N_S5)
    for x in ("dt", "lr", "mag", "mag8", "ang", "sin", "half", "cos", "are", "aim", "den", "fre", "fim", "ta", "tb", "turns"):
        put(x, S_PAIRS)
    z["turns"] = z["turns"].bitcast(I32)
    put("pw", CH + 1, S_PAIRS, n=2)
    put("pr", CH, S_PAIRS, n=2)
    put("ph_b", S_PAIRS, 16, n=2)
    put("ph_a", S_PAIRS, 9, n=2)
    put("tmp", S_PAIRS * G_CH, n=2)
    put("ph", QP, 144, n=2)
    put("m", QP, P, n=2)
    put("win", QP, P, n=2)
    put("cc", QP, G_CH, n=2)
    put("k", P)
    put("t", GPT, P)
    put("wout", QP, P, n=2)
    put("u", GPT, NJ)
    put("h", T)
    put("v", QP, NJ, n=2)
    put("x", QP, NJ + 1, n=2)
    z["yh"], z["y"] = carve(0, T), carve(T, GPT, NJ)
    put("m8", QP, NJ)
    z["end"] = at
    return z


def stream_uses(name, key):
    n = 0
    for phase, count, slots in STREAM:
        if phase == name:
            return n
        n += count * sum(1 for s in slots if key(s))
    return n


def first_slab(name):
    return stream_uses(name, lambda s: True)


def slots_of(name):
    return next((n, s) for phase, n, s in STREAM if phase == name)


def trunk(nc, xT, wstream, small_in, const_in, s5_in, outT):
    with ExitStack() as ctx:
        def sb(name, shape, dt=F32):
            return ctx.enter_context(nc.sbuf_tensor(name, shape, dt))

        def sem(name):
            return ctx.enter_context(nc.semaphore(name))

        resid = [nc.dram_tensor(f"resid{i}", (P, KT, T), F32, kind="Internal").ap() for i in range(3)]
        proj = nc.dram_tensor("proj", (N_PROJ, P, T_PAD), F32, kind="Internal").ap()
        s5_u = nc.dram_tensor("s5_u", (KT, CH, P, NJ), F32, kind="Internal").ap()
        s5_y = nc.dram_tensor("s5_y", (KT, CH, P, NJ), F32, kind="Internal").ap()

        x_hi = sb("x_hi", [P, KT, T], F32R)
        x_lo = sb("x_lo", [P, KT, T], F32R)
        act_hi = sb("act_hi", [P, 2, T], F32R)
        act_lo = sb("act_lo", [P, 2, T], F32R)
        w_hi = sb("w_hi", [P, SLOTS, 1024], F32R)
        w_lo = sb("w_lo", [P, SLOTS, 1024], F32R)
        stage = sb("stage", [P, 2, 1024])
        small = sb("small", [P, N_SMALL])
        const = sb("const", [P, N_CONST])
        AREA = 19000
        area = sb("area", [P, AREA])

        def carve(at, *shape):
            n = int(np.prod(shape))
            assert at + n <= AREA, (at, n)
            v = area[:, at:at + n]
            if len(shape) == 2:
                v = v.rearrange("p (a b) -> p a b", a=shape[0])
            if len(shape) == 3:
                v = v.rearrange("p (a b c) -> p a b c", a=shape[0], b=shape[1])
            return v

        bank = [ctx.enter_context(nc.psum_tensor(f"bank{i}", [P, 512], F32)) for i in range(8)]

        ident = const[:, C_ID:C_ID + P]
        ones = const[:, C_ONES:C_ONES + P]
        incl = const[:, C_INCL:C_INCL + P]
        strict = const[:, C_STRICT:C_STRICT + P]

        def level(n):
            return const[:, C_LEVEL + P * n:C_LEVEL + P * n + P]

        def over_heads(m):
            return m.rearrange("p (a c) -> p a c", a=1).to_broadcast([P, HEADS, P])

        def h4(v):
            return v.rearrange("p (h c) -> p h c", h=HEADS)

        stage_loaded = [sem(f"stage_loaded{i}") for i in range(2)]
        split_done = sem("split_done")
        high_split = sem("high_split")

        params_loaded = sem("params_loaded")
        zeros_written = sem("zeros_written")
        x_ready = sem("x_ready")
        group_done = sem("group_done")
        group_free = sem("group_free")
        nm_loaded = [sem(f"nm_loaded{i}") for i in range(2)]
        nm_square = sem("nm_square")
        nm_root = sem("nm_root")
        nm_recip = sem("nm_recip")
        nm_resid = sem("nm_resid")
        nm_normed = sem("nm_normed")
        nm_high = sem("nm_high")
        nm_sum = sem("nm_sum")
        nm_stored = [sem(f"nm_stored{i}") for i in range(2)]
        gate_dve = sem("gate_dve")
        gate_act = sem("gate_act")
        conv_done = sem("conv_done")
        glu_gate = sem("glu_gate")
        glu_mul = sem("glu_mul")
        proj_out = sem("proj_out")
        proj_stored = [sem(f"proj_stored{i}") for i in range(2)]
        cols_done = sem("cols_done")
        cols_ready = sem("cols_ready")
        dn = {k: sem("dn_" + k) for k in (
            "qkv_loaded0", "qkv_loaded1", "z_loaded0", "z_loaded1", "squares", "bcast", "scales",
            "kq", "qd", "vt", "expo", "kk", "decay", "inputs_used", "ident_minus", "x_t", "x0", "masked", "p", "p_sb",
            "up", "x_new", "u_t", "u_sb", "ks", "rhs", "vn", "vn_sb", "o", "state", "o_scale",
            "o_norm", "o_t", "o_gated", "o_hi", "out")}
        sk = {k: sem("sb_" + k) for k in (
            "loaded", "tail_group", "z", "soft", "logw", "w", "wm", "w_t", "wt_sb",
            "o", "o_hi", "o_lo")}
        gu_done = sem("gu_done")
        silu_done = sem("silu_done")
        act_f32 = sem("act_f32")
        act_high = sem("act_high")
        act_ready = sem("act_ready")
        down_done = sem("down_done")
        down_free = sem("down_free")
        s5 = {k: sem("s5_" + k) for k in (
            "angles", "t_done", "u_stored0", "u_stored1", "params", "act", "u_loaded", "h_loaded", "win", "win_t", "win_sb",
            "k", "k_sb", "t_sb", "v", "v_sb", "x", "y", "y_sb", "y_stored", "y_loaded", "skip",
            "gelu", "hi", "lo")}

        acc = carve(0, KT, T)
        A1 = KT * T

        nv = norm_views(carve, A1)

        def norm_bank(r, c, m):
            return bank[7 if r == 0 else c if r == 4 else NORM_ORDER.index((c, m))]

        acc_complete = {1: (group_free, 6 + GROUPS_BEFORE["ssm_in"]), 2: (down_free, 4 + 24 * PAIRS),
                        3: (glu_mul, 3 + 24), 4: (down_free, 4 + 48 * PAIRS)}
        sb_eps = sb("sb_eps", [P, 4])
        eps_ready = sem("eps_ready")
        gate_col = sb_eps[:, 2:3]
        act_chain_sem = sem("act_chain")
        dve_chain_sem = sem("dve_chain")

        def last_reader(name, i, slot):
            if name.startswith("ffn"):
                turn = int(name[3:]) * PAIRS + i
                return (gu_done, turn * 6 + 3 * (slot // 2) + 3) if slot < 4 else (down_done, turn * 24 + 25)
            if name == "gates":
                return group_done, len(HALF_CUTS)
            at = GROUPS_BEFORE[name] + i * 12
            return group_done, at + (6 * (slot // 2) + 6 if name == "glu" else 3 * slot + 3)

        def split_value(name, i, j):
            return first_slab(name) + i * len(slots_of(name)[1]) + j + 3

        block = ctx.enter_context(nc.Block())

        @block.sync
        def _(sp):
            for name, count, slots in STREAM:
                base = first_slab(name)

                def load(i, name=name, slots=slots, base=base):
                    for j, slot in enumerate(slots):
                        n = base + i * len(slots) + j
                        sp.wait_ge(split_done, n + 1)
                        sp.dma_start(stage[:, slot % 2, :], wstream[n]).then_inc(stage_loaded[slot % 2], 16)
                if count == 1:
                    load(0)
                else:
                    with sp.Fori(0, count) as i:
                        load(i)

        @block.gpsimd
        def _(pool):
            for _i in range(2):
                pool.sem_inc(split_done, 1)
            last_of = {}

            def split(name, slots, i, before):
                for j, slot in enumerate(slots):
                    h = slot % 2
                    same = [s for s in slots if s % 2 == h]
                    use = stream_uses(name, lambda s: s % 2 == h) + i * len(same) + same.index(slot)
                    n = first_slab(name) + i * len(slots) + j
                    pool.wait_ge(stage_loaded[h], (use + 1) * 16)
                    if before is not None:
                        pool.wait_ge(*last_reader(before, i - 1, slot))
                    elif slot in last_of:
                        pool.wait_ge(*last_reader(*last_of[slot], slot))
                    per_block = lambda w: w.rearrange("p (k c) -> p k c", c=P)
                    pool.tensor_tensor(per_block(w_hi[:, slot, :]), per_block(stage[:, h, :]), all_ones, ALU.mult
                                       ).then_inc(high_split, 1)
                    pool.wait_ge(high_split, n + 1)
                    pool.tensor_tensor(w_lo[:, slot, :], stage[:, h, :], w_hi[:, slot, :].bitcast(F32),
                                       ALU.subtract).then_inc(split_done, 1)

            all_ones = ones.rearrange("p (a c) -> p a c", a=1).to_broadcast([P, KT, P])
            pool.wait_ge(params_loaded, 32)
            for name, count, slots in STREAM:
                split(name, slots, 0, None)
                if count > 1:
                    with pool.Fori(1, count) as i:
                        split(name, slots, i, name)
                for slot in slots:
                    last_of[slot] = (name, count - 1)

        @block.tensor
        def _(pe):
            mm = pe.matmul

            def gemm(out, slot, k, xk, cut, first, last, hi=x_hi, lo=x_lo):
                a, n = cut
                wk = slice(k * P, k * P + P)
                mm(out[:, 0:n], w_hi[:, slot, wk], hi[:, xk, a:a + n], start=first, stop=False)
                mm(out[:, 0:n], w_hi[:, slot, wk], lo[:, xk, a:a + n], start=False, stop=False)
                return mm(out[:, 0:n], w_lo[:, slot, wk], hi[:, xk, a:a + n], start=False, stop=last)

            def tile_groups(name, i, group0, cuts=CUTS, x_from=None):
                _, slots = slots_of(name)
                for j, slot in enumerate(slots):
                    pe.wait_ge(split_done, split_value(name, i, j))
                    for c, cut in enumerate(cuts):
                        g = group0 + (i * len(slots) + j) * len(cuts) + c
                        b = bank[(j * len(cuts) + c) % 6]
                        pe.wait_ge(group_free, g + 1)
                        if x_from is not None and j == 0:
                            pe.wait_ge(x_ready, x_from(c))
                        for k in range(KT):
                            last = gemm(b, slot, k, k, cut, k == 0, k == KT - 1)
                        last.then_inc(group_done, 1)

            def pair_groups(i):
                _, slots = slots_of("glu")
                for j in range(0, len(slots), 2):
                    pe.wait_ge(split_done, split_value("glu", i, j + 1))
                    for c, cut in enumerate(CUTS):
                        for v in range(2):
                            if v == 0:
                                pe.wait_ge(glu_mul, i * 6 + 3 * (j // 2) + c + 1)
                            for k in range(KT):
                                last = gemm(bank[2 * c + v], slots[j + v], k, k, cut, k == 0, k == KT - 1)
                            last.then_inc(group_done, 1)

            def norm_sums(r):
                for c, m in norm_steps(r):
                    a, n = CUTS[c]
                    e = norm_event(r, c, m)
                    for k in range(KT):
                        if k % 4 == 0:
                            pe.wait_ge(nm_square, 2 * e + k // 4 + 1)
                        last = mm(norm_bank(r, c, m)[:, 0:n], ones, nv["sq"][:, k % 4, 0:n], start=(k == 0),
                                  stop=(k == KT - 1))
                        if k % 4 == 3:
                            last.then_inc(nm_sum, 1)

            def ffn(layer, x0):
                name = f"ffn{layer}"
                base = layer * PAIRS

                def pair(i, first):
                    for f in range(2):
                        g, u = 2 * f, 2 * f + 1
                        pe.wait_ge(split_done, split_value(name, i, u))
                        for c, cut in enumerate(CUTS):
                            b = 2 * ((3 * f + c) % 2)
                            step = (base + i) * 6 + 3 * f + c
                            pe.wait_ge(act_f32, step + 1)
                            if first and f == 0:
                                pe.wait_ge(x_ready, x0 + c + 1)
                            for s in (g, u):
                                for k in range(KT):
                                    last = gemm(bank[b + s % 2], s, k, k, cut, k == 0, k == KT - 1)
                            last.then_inc(gu_done, 1)
                    pe.wait_ge(split_done, split_value(name, i, 5))
                    for c, cut in enumerate(CUTS):
                        pe.wait_ge(act_ready, (base + i) * 6 + 3 + c + 1)
                        for m in range(KT):
                            pe.wait_ge(down_free, (base + i) * 24 + c * 8 + m + 1)
                            b = bank[4 + m % 4]
                            slot = 4 + m // 4
                            for kk in range(2):
                                last = gemm(b, slot, kk * 4 + m % 4, kk, cut, kk == 0, kk == 1, act_hi, act_lo)
                            last.then_inc(down_done, 1)

                pair(0, True)
                with pe.Fori(1, PAIRS) as i:
                    pair(i, False)

            for s_, k_ in ((sk["wt_sb"], 2), (sk["o"], 2), (sk["z"], 1)):
                for _i in range(k_):
                    pe.sem_inc(s_, 1)
            pe.wait_ge(params_loaded, 32)

            norm_sums(0)
            tile_groups("gates", 0, 0, HALF_CUTS, x_from=lambda c: c // 2 + 1)
            with pe.Fori(0, 7) as i:
                tile_groups("in_proj", i, 6)

            rows = carve(0, T_ROWS)
            pe.wait_ge(gate_dve, GATE_DVE)
            for n in range(BLOCKS):
                last = pe.transpose(bank[6 + n // 8][:, n % 8 * 64:n % 8 * 64 + 64], rows[0:64, n * P:n * P + P],
                                    ident[0:64, 0:64])
            last.then_inc(cols_done, 1)

            v = dn_views(carve)

            def dn_parallel(n, s):
                B = bank[4 * s:4 * s + 4]
                q, k, w, kb = (v[s][x] for x in ("q", "k", "v", "kb"))
                pe.wait_ge(dn["squares"], n + 1)
                pe.wait_ge(dn["out"], n + 1)
                mm(B[0][:], ones, v[s]["t1"], start=True, stop=True)
                mm(B[1][:], ones, v[s]["t2"], start=True, stop=True)
                for h in range(HEADS):
                    hs = slice(h * P, h * P + P)
                    sel_g = const[0:64, C_SEL + h * P:C_SEL + h * P + P]
                    sel_b = const[0:64, C_SEL + (4 + h) * P:C_SEL + (5 + h) * P]
                    mm(B[2][:, hs], sel_g, rows[0:64, bass.ts(n, P)], start=True, stop=True)
                    last = mm(B[3][:, hs], sel_b, rows[0:64, bass.ts(n, P)], start=True, stop=True)
                last.then_inc(dn["bcast"], 1)

            def dn_products(n, s):
                B = bank[4 * s:4 * s + 4]
                q, k, w, kb = (v[s][x] for x in ("q", "k", "v", "kb"))
                pe.wait_ge(dn["kq"], n + 1)
                pe.wait_ge(dn["scales"], n + 1)
                for h in range(HEADS):
                    hs = slice(h * P, h * P + P)
                    mm(B[0][:, hs], k[:, hs], kb[:, hs], start=True, stop=True)
                    mm(B[1][:, hs], k[:, hs], q[:, hs], start=True, stop=True)
                for h in range(HEADS):
                    hs = slice(h * P, h * P + P)
                    pe.transpose(B[3][:, hs], k[:, hs], ident)
                    last = pe.transpose(B[2][:, hs], w[:, hs], ident)
                last.then_inc(dn["kk"], 1)

            def dn_first(n, s):
                B = bank[4 * s:4 * s + 4]
                pe.wait_ge(dn["ident_minus"], n + 1)
                pe.wait_ge(dn["vt"], n + 1)
                for h in range(HEADS):
                    hs = slice(h * P, h * P + P)
                    last = pe.transpose(B[2][:, hs], v[s]["u"][:, hs], ident)
                last.then_inc(dn["x_t"], 1)

            def dn_level_p(n, s, at):
                B = bank[4 * s:4 * s + 4]
                pe.wait_ge(dn["masked"], at + 1)
                if s is not None:
                    pe.wait_ge(dn["x0"], n + 1)
                for h in range(HEADS):
                    hs = slice(h * P, h * P + P)
                    last = mm(B[0][:, hs], v[s]["t1"][:, hs], v[s]["x"][:, hs], start=True, stop=True)
                last.then_inc(dn["p"], 1)

            def dn_level_up(n, s, at):
                B = bank[4 * s:4 * s + 4]
                pe.wait_ge(dn["p_sb"], at + 1)
                for h in range(HEADS):
                    hs = slice(h * P, h * P + P)
                    last = mm(B[1][:, hs], v[s]["u"][:, hs], v[s]["t2"][:, hs], start=True, stop=True)
                last.then_inc(dn["up"], 1)

            def dn_level_t(n, s, at):
                B = bank[4 * s:4 * s + 4]
                pe.wait_ge(dn["x_new"], at + 1)
                for h in range(HEADS):
                    hs = slice(h * P, h * P + P)
                    last = pe.transpose(B[2][:, hs], v[s]["x"][:, hs], ident)
                last.then_inc(dn["u_t"], 1)

            def dn_state(n, s, lvl):
                B = bank[4 * s:4 * s + 4]
                pe.wait_ge(dn["state"], n + 1)
                pe.wait_ge(dn["u_sb"], lvl)
                for h in range(HEADS):
                    hs = slice(h * P, h * P + P)
                    last = mm(B[0][:, hs], v[s]["kb"][:, hs], v["state"][:, hs], start=True, stop=True)
                last.then_inc(dn["ks"], 1)
                pe.wait_ge(dn["rhs"], n + 1)
                for h in range(HEADS):
                    hs = slice(h * P, h * P + P)
                    last = mm(B[1][:, hs], v[s]["u"][:, hs], v[s]["t1"][:, hs], start=True, stop=True)
                last.then_inc(dn["vn"], 1)
                pe.wait_ge(dn["vn_sb"], n + 1)
                for h in range(HEADS):
                    hs = slice(h * P, h * P + P)
                    mm(B[2][:, hs], v[s]["qd"][:, hs], v["state"][:, hs], start=True, stop=False)
                    mm(B[2][:, hs], v[s]["qk"][:, hs], v[s]["t2"][:, hs], start=False, stop=True)
                for h in range(HEADS):
                    hs = slice(h * P, h * P + P)
                    last = mm(B[3][:, hs], v[s]["kd"][:, hs], v[s]["t2"][:, hs], start=True, stop=True)
                last.then_inc(dn["o"], 1)

            def dn_out(n, s):
                B = bank[4 * s:4 * s + 4]
                pe.wait_ge(dn["o_norm"], n + 1)
                for h in range(HEADS):
                    hs = slice(h * P, h * P + P)
                    last = pe.transpose(B[0][:, hs], v[s]["x"][:, hs], ident)
                last.then_inc(dn["o_t"], 1)

            def dn_blocks(n0, sets):
                for s in range(sets):
                    dn_parallel(n0 + s, s)
                for s in range(sets):
                    dn_products(n0 + s, s)
                for s in range(sets):
                    dn_first(n0 + s, s)
                for lev in range(1, LEVELS):
                    at = n0 * (LEVELS - 1) + (lev - 1) * sets
                    for s in range(sets):
                        dn_level_p(n0 + s, s, at + s)
                    for s in range(sets):
                        dn_level_up(n0 + s, s, at + s)
                    for s in range(sets):
                        dn_level_t(n0 + s, s, at + s)
                for s in range(sets):
                    dn_state(n0 + s, s, (n0 + sets) * (LEVELS - 1))
                for s in range(sets):
                    dn_out(n0 + s, s)

            pe.wait_ge(cols_ready, 1)
            with pe.Fori(0, (BLOCKS - 1) // 2) as i:
                dn_blocks(2 * i, 2)
            dn_blocks(BLOCKS - 1, 1)

            sv = sb_views(carve)
            pe.wait_ge(dn["out"], BLOCKS + 2)

            def sb_head(hd):
                w0 = hd * WT_GROUPS
                pe.wait_ge(sk["loaded"], 48 * (hd + 1))
                for g in range(3):
                    js = range(4 * g, min(4 * g + 4, BLOCKS))
                    pe.wait_ge(sk["wt_sb"], w0 + g + 1)
                    for j in js:
                        n = min(P, T - j * P)
                        last = pe.transpose(bank[4 + g % 2][0:n, j % 4 * P:j % 4 * P + P],
                                            sv["v"][:, j * P:j * P + n], ident)
                    last.then_inc(sk["w_t"], 1)

                for i in range(BLOCKS + 2):
                    if i < BLOCKS:
                        nq, nk = min(P, T - i * P), min(T, (i + 1) * P)
                        pe.wait_ge(sk["logw"], hd * BLOCKS + i + (1 if 0 < i < BLOCKS - 1 else 2))
                        for a in range(0, nk, 512):
                            m = min(512, nk - a)
                            last = mm(bank[(2 * (i % 2) + a // 512) % 4][0:nq, 0:m], sv["q"][:, i * P:i * P + nq],
                                      sv["k"][:, a:a + m], start=True, stop=True)
                        last.then_inc(sk["z"], 1)
                    if i > 1:
                        sb_out(hd, i - 2, w0)

            def sb_out(hd, i, w0):
                nq, nk = min(P, T - i * P), min(T, (i + 1) * P)
                pe.wait_ge(sk["wm"], hd * BLOCKS + i + 1)
                groups = [range(a, min(a + 4, i + 1)) for a in range(0, i + 1, 4)]
                base = w0 + 3 + WT_BEFORE[i]
                for gi, js in enumerate(groups):
                    g = base + gi
                    pe.wait_ge(sk["wt_sb"], g + 1)
                    if i == BLOCKS - 1:
                        pe.sem_inc(sk["tail_group"], 1)
                    for j in js:
                        n = min(P, T - j * P)
                        last = pe.transpose(bank[4 + (3 + WT_BEFORE[i] + gi) % 2][0:n, j % 4 * P:j % 4 * P + nq],
                                            sv["e"][i % 3][0:nq, j * P:j * P + n], ident[0:nq, 0:nq])
                    last.then_inc(sk["w_t"], 1)
                pe.wait_ge(sk["wt_sb"], base + len(groups) + 2)
                pe.wait_ge(sk["o_lo"], hd * BLOCKS + i + (1 if i > 0 else 2))
                for j in range(i + 1):
                    n = min(P, T - j * P)
                    last = mm(bank[6 + i % 2][:, 0:nq], sv["vt"][0:n, j * P:j * P + P], sv["wt"][0:n, j, 0:nq],
                              start=(j == 0), stop=(j == i))
                last.then_inc(sk["o"], 1)

            with pe.Fori(0, HEADS) as hd:
                sb_head(hd)

            pe.wait_ge(sk["o_lo"], HEADS * BLOCKS + 2)
            with pe.Fori(0, 2) as i:
                tile_groups("w_out", i, GROUPS_BEFORE["w_out"])
            norm_sums(1)
            ffn(0, 3)
            norm_sums(2)
            pe.wait_ge(x_ready, 9)
            with pe.Fori(0, 2) as i:
                tile_groups("ssm_in", i, GROUPS_BEFORE["ssm_in"])

            z = s5_views(carve)

            def s5_tile(m):
                pe.wait_ge(s5["win"], m + 1)
                for part in range(2):
                    for q in range(QP):
                        last = pe.transpose(bank[part][:, q * P:q * P + P], z["m"][part][:, q, :], ident)
                last.then_inc(s5["win_t"], 1)
                for q in range(QP):
                    for b in range(2):
                        r = slice(STATE * b, STATE * b + STATE)
                        o = bank[2 + b][:, q * G_CH:q * G_CH + G_CH]
                        mm(o, z["m"][0][r, q, :], z["cc"][0][r, q, :],
                           start=True, stop=False)
                        last = mm(o, z["m"][1][r, q, :], z["cc"][1][r, q, :], start=False, stop=True)
                last.then_inc(s5["k"], 1)
                pe.wait_ge(s5["k_sb"], m + 1)
                for t in range(CH):
                    off = C_SHIFT + G_CH * (CH - 1 - t)
                    last = mm(bank[4 + t // 4][:, t % 4 * P:t % 4 * P + P], const[:, off:off + P], z["k"],
                              start=True, stop=True)
                last.then_inc(s5["t_done"], 1)
                pe.wait_ge(s5["win_sb"], m + 1)
                pe.wait_ge(s5["u_loaded"], (m + 1) * (16 * CH))
                for part in range(2):
                    for q in range(QP):
                        for b in range(2):
                            r = slice(STATE * b, STATE * b + STATE)
                            o = bank[2 * part + q // 2][r, q % 2 * NJ:q % 2 * NJ + NJ]
                            last = mm(o, z["win"][part][:, q, r], z["u"][:, 2 * q + b, :], start=True, stop=True)
                last.then_inc(s5["v"], 1)
                pe.wait_ge(s5["t_sb"], m + 1)
                pe.wait_ge(s5["x"], m + 1)
                for q in range(QP):
                    for b in range(2):
                        r = slice(STATE * b, STATE * b + STATE)
                        o = bank[4 + 2 * (q // 2) + b][:, q % 2 * NJ:q % 2 * NJ + NJ]
                        mm(o, z["t"][:, 2 * q + b, :], z["u"][:, 2 * q + b, :], start=True, stop=False)
                        mm(o, z["wout"][0][r, q, :], z["x"][0][r, q, 0:NJ], start=False, stop=False)
                        last = mm(o, z["wout"][1][r, q, :], z["x"][1][r, q, 0:NJ], start=False, stop=True)
                last.then_inc(s5["y"], 1)

            with pe.Fori(0, KT) as m:
                s5_tile(m)
            pe.wait_ge(s5["lo"], KT)
            with pe.Fori(0, 4) as i:
                pair_groups(i)
            norm_sums(3)
            ffn(1, 9)
            norm_sums(4)

        @block.scalar
        def _(act):
            A = nc.scalar.activation
            eps_col = sb_eps[:, 0:1]
            ch = Chain(act, act_chain_sem)

            def residual_block(r, src, dst):
                def load(c):
                    a, n = CUTS[c]
                    p = 3 * r + c
                    if c >= 2:
                        act.wait_ge(*([nm_normed, p - 1] if r < 4 else [nm_resid, p - 1 - 3]))
                        if r > 0:
                            act.wait_ge(nm_stored[0], 16 * (2 * (r - 1) + 1))
                    act.dma_start(nv["h"][c % 2][:, :, 0:n], src[:, :, a:a + n]).then_inc(nm_loaded[c % 2], 16)

                def square(c, m):
                    a, n = CUTS[c]
                    if r == 0:
                        act.wait_ge(nm_loaded[c % 2], 16 * (c // 2 + 1))
                    e = norm_event(r, c, m)
                    x = nv["h"][c % 2][:, :, 0:n] if m else acc[:, :, a:a + n]
                    for half in range(2):
                        if e + half:
                            act.wait_ge(nm_sum, 2 * e + half)
                        A(nv["sq"][:, :, 0:n], x[:, 4 * half:4 * half + 4], ACT.Square).then_inc(nm_square, 1)

                def root(c, m):
                    n = CUTS[c][1]
                    e = norm_event(r, c, m)
                    act.wait_ge(nm_sum, 2 * e + 2)
                    if r > 0:
                        at = norm_steps(r).index((c, m))
                        if at >= 2:
                            c2, m2 = norm_steps(r)[at - 2]
                            act.wait_ge(*((nm_normed, 3 * r + c2 + 1) if m2 else (nm_resid, 3 * (r - 1) + c2 + 1)))
                    elif c == 2:
                        act.wait_ge(nm_normed, 1)
                    A(nv["rs"][e % 2][:, 0:n], norm_bank(r, c, m)[:, 0:n], ACT.Sqrt, scale=1.0 / D, bias=eps_col
                      ).then_inc(nm_root, 1)

                def store(c):
                    a, n = CUTS[c]
                    act.wait_ge(nm_resid, 3 * (r - 1) + c + 1)
                    skip = N_META if (r == 4 and c == 0) else 0
                    o = a - N_META if r == 4 else a
                    act.dma_start(dst[:, :, o + skip:o + n], nv["h"][c % 2][:, :, skip:n]).then_inc(nm_stored[c % 2], 16)

                def high(c):
                    a, n = CUTS[c]
                    act.wait_ge(nm_normed, 3 * r + c + 1)
                    A(x_hi[:, :, a:a + n], nv["nb"][:, :, 0:n], ACT.Copy).then_inc(nm_high, 1)

                load(0)
                load(1)
                if r == 0:
                    square(0, 1)
                    root(0, 1)
                    square(1, 1)
                    high(0)
                    root(1, 1)
                    load(2)
                    high(1)
                    square(2, 1)
                    root(2, 1)
                    high(2)
                    return
                act.wait_ge(*acc_complete[r])
                square(0, 0)
                root(0, 0)
                square(1, 0)
                if r == 4:
                    root(1, 0)
                    square(2, 0)
                    store(0)
                    load(2)
                    root(2, 0)
                    store(1)
                    store(2)
                    return
                root(1, 0)
                store(0)
                square(0, 1)
                root(0, 1)
                square(2, 0)
                root(2, 0)
                store(1)
                high(0)
                load(2)
                square(1, 1)
                root(1, 1)
                high(1)
                store(2)
                square(2, 1)
                root(2, 1)
                high(2)

            act.dma_start(small[:], small_in).then_inc(params_loaded, 16)
            act.dma_start(const[:], const_in).then_inc(params_loaded, 16)
            act.wait_ge(eps_ready, 3)
            zeros = carve(18300, T_PAD - T)
            for g in range(4):
                act.dma_start(proj[7 * g:7 * g + 7, :, T:T_PAD].rearrange("m p t -> p m t"),
                              zeros.rearrange("p (a t) -> p a t", a=1).to_broadcast([P, 7, T_PAD - T])
                              ).then_inc(zeros_written, 16)
            for _i in range(6):
                act.sem_inc(group_free, 1)
            for i in range(2):
                act.sem_inc(proj_stored[i], 16)
                act.sem_inc(s5[f"u_stored{i}"], 16)
            act.wait_ge(params_loaded, 32)
            residual_block(0, xT, None)

            rows = carve(0, T_ROWS)
            ga, gb = carve(T_ROWS, T_ROWS), carve(2 * T_ROWS, T_ROWS)
            act.wait_ge(nm_normed, 3)
            ch(A(gate_col[0:4, :], small[0:4, A_LOG:A_LOG + 1], ACT.Exp))
            act.wait_ge(gate_dve, 1)
            for c, (a, n) in enumerate(HALF_CUTS):
                act.wait_ge(group_done, c + 1)
                A(rows[32:36, a:a + n], bank[c][32:36, 0:n], ACT.Exp, scale=-1.0)
                A(ga[0:4, a:a + n], bank[c][0:4, 0:n], ACT.Identity, bias=small[0:4, DT_BIAS:DT_BIAS + 1]
                  ).then_inc(group_free, 1)
            act.wait_ge(group_free, 6 + 6)
            ch(A(gb[0:4, 0:T], ga[0:4, 0:T], ACT.Abs))
            ch.sync()
            ch(A(gb[0:4, 0:T], gb[0:4, 0:T], ACT.Exp, scale=-1.0))
            ch.sync()
            A(gb[0:4, 0:T], gb[0:4, 0:T], ACT.Ln, bias=1.0).then_inc(gate_act, 1)

            cb, ct, po = conv_views(carve)

            def proj_store(u, s):
                act.dma_start(proj[u][:, 0:T], po[s % 2]).then_inc(proj_stored[s % 2], 16)

            def conv_tiles(i):
                for s in range(4):
                    u = 4 * i + s
                    par = s % 2
                    act.wait_ge(conv_done, u + 1)
                    for c, (a, n) in enumerate(CUTS):
                        act.wait_ge(group_done, 6 + 3 * u + c + 1)
                        A(cb[par][:, 3 + a:3 + a + n], bank[(3 * s + c) % 6][:, 0:n], ACT.Copy).then_inc(group_free, 1)
                    act.wait_ge(conv_done, u + 3)
                    act.wait_ge(proj_stored[par], (2 * i + s // 2 + 1) * 16)
                    A(po[par], ct[par], ACT.Silu).then_inc(proj_out, 1)
                    act.wait_ge(proj_out, u + 3)
                    proj_store(u, s)

            def plain_tiles(i, func, scale=1.0):
                for s in range(4):
                    u = 4 * i + s
                    par = s % 2
                    act.wait_ge(proj_stored[par], (2 * i + s // 2 + 1) * 16)
                    for c, (a, n) in enumerate(CUTS):
                        act.wait_ge(group_done, 6 + 3 * u + c + 1)
                        last = A(po[par][:, a:a + n], bank[(3 * s + c) % 6][:, 0:n], func, scale=scale)
                        last.then_inc(group_free, 1)
                    act.wait_ge(group_free, 6 + 6 + 3 * u + 3)
                    proj_store(u, s)

            with act.Fori(0, 3) as i:
                conv_tiles(i)
            plain_tiles(3, ACT.Silu)
            plain_tiles(4, ACT.Copy, HD ** -0.5)
            with act.Fori(5, 7) as i:
                plain_tiles(i, ACT.Copy)

            v = dn_views(carve)
            nc.scalar.preload_act_table_set("natural_log_exp_and_others")
            for i in range(2):
                act.wait_ge(proj_stored[i], 16 * 15)
            act.wait_ge(zeros_written, 64)
            act.wait_ge(cols_done, 1)
            A(v["cols"][:, 0:8, :].rearrange("p a b -> p (a b)"), bank[6][:], ACT.Copy)
            A(v["cols"][:, 8, :], bank[7][:, 0:64], ACT.Copy).then_inc(cols_ready, 1)

            def dn_load(n, s, z):
                for m, x in ([(DZ, "z")] if z else [(DQ, "q"), (DK, "k"), (DV, "v")]):
                    act.dma_start(h4(v[s][x]), proj[m:m + 4, :, bass.ts(n, P)].rearrange("m p t -> p m t")
                                  ).then_inc(dn[("z" if z else "qkv") + f"_loaded{s}"], 16)

            act.wait_ge(gate_dve, GATE_DVE)
            for s in range(2):
                dn_load(s, s, False)
                dn_load(s, s, True)

            def dn_act_blocks(n0, i, sets, width=P):
                for s in range(sets):
                    act.wait_ge(dn[f"qkv_loaded{s}"], 48 * (i + 1))
                    act.wait_ge(dn["out"], n0 + s + 1)
                    A(v[s]["t1"], v[s]["k"], ACT.Square)
                    A(v[s]["t2"], v[s]["q"], ACT.Square).then_inc(dn["squares"], 1)
                for s in range(sets):
                    n, B = n0 + s, bank[4 * s:4 * s + 4]
                    act.wait_ge(dn["bcast"], n + 1)
                    A(v[s]["t1"], B[0][:], ACT.Ln, bias=eps_col)
                    ch(A(v[s]["t2"], B[1][:], ACT.Ln, scale=float(HD), bias=sb_eps[:, 1:2]))
                    ch.sync()
                    A(v[s]["t1"], v[s]["t1"], ACT.Exp, scale=-0.5)
                    A(v[s]["t2"], v[s]["t2"], ACT.Exp, scale=-0.5)
                    act.wait_ge(dn["expo"], n + 1)
                    A(v[s]["eg"], B[2][:], ACT.Exp).then_inc(dn["scales"], 1)
                    A(v[s]["lt"], v[s]["lt"], ACT.Exp)
                    A(v[s]["ecol"], v[s]["ecol"], ACT.Exp).then_inc(dn["decay"], 1)
                for s in range(sets):
                    n, B = n0 + s, bank[4 * s:4 * s + 4]
                    act.wait_ge(dn["kk"], n + 1)
                    A(v[s]["vt"], B[2][:], ACT.Copy).then_inc(dn["vt"], 1)
                for s in range(sets):
                    n, B = n0 + s, bank[4 * s:4 * s + 4]
                    act.wait_ge(dn["x_t"], n + 1)
                    A(v[s]["x"], B[2][:], ACT.Copy).then_inc(dn["x0"], 1)
                if sets == 2:
                    for s in range(2):
                        act.wait_ge(dn["inputs_used"], n0 + s + 1)
                        dn_load(n0 + 2 + s, s, False)
                for lev in range(1, LEVELS):
                    at = n0 * (LEVELS - 1) + (lev - 1) * sets
                    for s in range(sets):
                        act.wait_ge(dn["p"], at + s + 1)
                        A(v[s]["t2"], bank[4 * s][:], ACT.Copy).then_inc(dn["p_sb"], 1)
                    for s in range(sets):
                        act.wait_ge(dn["u_t"], at + s + 1)
                        A(v[s]["u"], bank[4 * s + 2][:], ACT.Copy).then_inc(dn["u_sb"], 1)
                for s in range(sets):
                    n, B = n0 + s, bank[4 * s:4 * s + 4]
                    act.wait_ge(dn["vn"], n + 1)
                    A(v[s]["t2"], B[1][:], ACT.Copy).then_inc(dn["vn_sb"], 1)
                    act.wait_ge(dn["o"], n + 1)
                    for h in range(HEADS):
                        hs = slice(h * P, h * P + P)
                        last = A(v[s]["x"][:, hs], B[2][:, hs], ACT.Square, accum_out=v[s]["ss"][:, h:h + 1])
                    ch(last)
                    ch.sync()
                    ch(A(v[s]["ss"], v[s]["ss"], ACT.Ln, scale=1.0 / HD, bias=eps_col))
                    ch.sync()
                    A(v[s]["ss"], v[s]["ss"], ACT.Exp, scale=-0.5).then_inc(dn["o_scale"], 1)
                for s in range(sets):
                    n = n0 + s
                    act.wait_ge(dn["o_gated"], n + 1)
                    A(x_hi[:, 0:HEADS, bass.ds(n * P, width)], h4(v[s]["t1"])[:, :, 0:width], ACT.Copy
                      ).then_inc(dn["o_hi"], 1)
                    if sets == 2:
                        dn_load(n0 + 2 + s, s, True)

            with act.Fori(0, (BLOCKS - 1) // 2) as i:
                ch.enter(i, 0, 6)
                dn_act_blocks(2 * i, i, 2)
            ch.leave((BLOCKS - 1) // 2)
            dn_act_blocks(BLOCKS - 1, (BLOCKS - 1) // 2, 1, TAIL)
            act.wait_ge(dn["qkv_loaded1"], 48 * 5)
            act.wait_ge(dn["z_loaded1"], 16 * 5)

            sv = sb_views(carve)
            act.wait_ge(dn["out"], BLOCKS + 2)

            def sb_head(hd):
                act.wait_ge(sk["z"], hd * BLOCKS + 1)
                for m, x in ((SQ, "q"), (SK, "k"), (SV, "v")):
                    act.dma_start(sv[x], proj[m + hd][:, 0:T]).then_inc(sk["loaded"], 16)
                w0 = hd * WT_GROUPS
                for g in range(3):
                    act.wait_ge(sk["w_t"], w0 + g + 1)
                    k = slice(0, P) if g < 2 else slice(0, TAIL)
                    w = 4 * P if g < 2 else P
                    A(sv["vt"][k, 4 * g * P:4 * g * P + w], bank[4 + g % 2][k, 0:w], ACT.Copy).then_inc(sk["wt_sb"], 1)
                for i in range(BLOCKS + 2):
                    if i < BLOCKS:
                        nq, nk = min(P, T - i * P), min(T, (i + 1) * P)
                        e = sv["e"][i % 3]
                        act.wait_ge(sk["z"], hd * BLOCKS + i + 2)
                        act.wait_ge(sk["o"], hd * BLOCKS + max(i, 1))
                        for a in range(0, nk, 512):
                            m = min(512, nk - a)
                            last = A(e[0:nq, a:a + m], bank[(2 * (i % 2) + a // 512) % 4][0:nq, 0:m], ACT.Abs)
                        ch(last)
                        ch.sync()
                        ch(A(e[0:nq, 0:nk], e[0:nq, 0:nk], ACT.Exp, scale=-1.0))
                        ch.sync()
                        A(e[0:nq, 0:nk], e[0:nq, 0:nk], ACT.Ln, bias=1.0).then_inc(sk["soft"], 1)
                    if 0 < i <= BLOCKS:
                        nq, nk = min(P, T - (i - 1) * P), min(T, i * P)
                        e = sv["e"][(i - 1) % 3]
                        act.wait_ge(sk["logw"], hd * BLOCKS + i + 2)
                        A(e[0:nq, 0:nk], e[0:nq, 0:nk], ACT.Exp).then_inc(sk["w"], 1)
                    if i > 1:
                        sb_evac(hd, i - 2, w0)

            def sb_evac(hd, i, w0):
                nq = min(P, T - i * P)
                for gi, j0 in enumerate(range(0, i + 1, 4)):
                    nj = min(4, i + 1 - j0)
                    act.wait_ge(sk["w_t"], w0 + 3 + WT_BEFORE[i] + gi + 1)
                    if gi == 0:
                        act.wait_ge(sk["o"], hd * BLOCKS + i + 2)
                    src = bank[4 + (3 + WT_BEFORE[i] + gi) % 2]
                    k = slice(0, TAIL) if j0 == BLOCKS - 1 else slice(0, P)
                    A(sv["wt"][k, j0:j0 + nj, 0:nq],
                      src[k, 0:nj * P].rearrange("p (j q) -> p j q", j=nj)[:, :, 0:nq], ACT.Copy).then_inc(sk["wt_sb"], 1)
                act.wait_ge(sk["o"], hd * BLOCKS + i + 3)
                A(x_hi[:, HEADS + hd, i * P:i * P + nq], bank[6 + i % 2][:, 0:nq], ACT.Copy).then_inc(sk["o_hi"], 1)

            with act.Fori(0, HEADS) as hd:
                ch.enter(hd, 0, 2 * BLOCKS)
                sb_head(hd)
            ch.leave(HEADS)

            act.wait_ge(sk["o_lo"], HEADS * BLOCKS + 2)
            with act.Fori(0, 2) as i:
                for s in range(4):
                    for c, (a, n) in enumerate(CUTS):
                        act.wait_ge(group_done, GROUPS_BEFORE["w_out"] + 12 * i + 3 * s + c + 1)
                        last = A(acc[:, 4 * i + s, a:a + n], bank[(3 * s + c) % 6][:, 0:n], ACT.Copy)
                        last.then_inc(group_free, 1)
            residual_block(1, xT, resid[0])

            def ffn(layer):
                base = layer * PAIRS
                gate, f = ffn_views(carve)
                act.wait_ge(nm_stored[0], 16 * (2 + 4 * layer))
                act.wait_ge(nm_stored[1], 16 * (1 + 2 * layer))
                with act.Fori(0, PAIRS) as i:
                    for st in range(6):
                        a, n = CUTS[st % 3]
                        step = (base + i) * 6 + st
                        act.wait_ge(gu_done, step + 1)
                        act.wait_ge(act_f32, step + 1)
                        A(gate[st % 2][:, 0:n], bank[2 * (st % 2)][:, 0:n], ACT.Silu).then_inc(silu_done, 1)
                        act.wait_ge(act_f32, step + 3)
                        act.wait_ge(down_done, (base + i) * 24 + 1)
                        A(act_hi[:, st // 3, a:a + n], f[st % 2][:, 0:n], ACT.Copy).then_inc(act_high, 1)
                act.wait_ge(act_ready, 6 * (base + PAIRS))

            act.sem_inc(down_done, 1)
            ffn(0)
            residual_block(2, resid[0], resid[1])

            z = s5_views(carve)
            act.wait_ge(x_ready, 9)
            act.wait_ge(nm_stored[0], 16 * 4)
            act.wait_ge(nm_stored[1], 16 * 2)
            with act.Fori(0, 2) as i:
                for s in range(4):
                    par = s % 2
                    act.wait_ge(s5[f"u_stored{par}"], (2 * i + s // 2 + 1) * 16)
                    for c, (a, n) in enumerate(CUTS):
                        act.wait_ge(group_done, GROUPS_BEFORE["ssm_in"] + 12 * i + 3 * s + c + 1)
                        last = A(z["ut"][par].rearrange("p (s j) -> p j s", s=CH)[:, a // CH:(a + n) // CH, :],
                                 bank[(3 * s + c) % 6][:, 0:n].rearrange("p (j s) -> p j s", s=CH), ACT.Copy)
                        last.then_inc(group_free, 1)
                    act.wait_ge(group_free, 6 + GROUPS_BEFORE["ssm_in"] + 12 * i + 3 * s + 3)
                    act.dma_start(s5_u[4 * i + s].rearrange("s c j -> c s j"),
                                  z["ut"][par].rearrange("p (s j) -> p s j", s=CH)).then_inc(s5[f"u_stored{par}"], 16)
            for i in range(2):
                act.wait_ge(s5[f"u_stored{i}"], 16 * 5)
            act.dma_start(z["par"], s5_in).then_inc(s5["params"], 16)
            act.wait_ge(s5["params"], 16)
            A(z["dt"], z["par"][:, S_LOG:S_LOG + 32], ACT.Exp).then_inc(s5["act"], 1)
            act.wait_ge(s5["angles"], 1)
            A(z["mag"], z["lr"], ACT.Exp)
            A(z["mag8"], z["lr"], ACT.Exp, scale=float(CH))
            A(z["sin"], z["ang"], ACT.Sin)
            A(z["half"], z["ang"], ACT.Sin, scale=0.5).then_inc(s5["act"], 1)

            def s5_tile(m):
                act.wait_ge(s5["y"], m + 1)
                act.wait_ge(s5["skip"], m + 1)
                for t in range(CH):
                    act.dma_start(z["u"][t * G_CH:t * G_CH + G_CH],
                                  s5_u[m, t].rearrange("(g c) j -> c g j", g=GPT)).then_inc(s5["u_loaded"], 16)
                act.dma_start(z["h"].rearrange("p (s j) -> p s j", s=CH),
                              s5_u[m].rearrange("s c j -> c s j")).then_inc(s5["h_loaded"], 16)
                act.wait_ge(s5["win_t"], m + 1)
                for part in range(2):
                    last = A(z["win"][part].rearrange("p q s -> p (q s)"), bank[part][:], ACT.Copy)
                last.then_inc(s5["win_sb"], 1)
                act.wait_ge(s5["k"], m + 1)
                for b in range(2):
                    last = A(z["k"].rearrange("p (q b c) -> p q b c", q=QP, b=2)[:, :, b, :],
                             bank[2 + b][:, 0:QP * G_CH].rearrange("p (q c) -> p q c", q=QP), ACT.Copy)
                last.then_inc(s5["k_sb"], 1)
                act.wait_ge(s5["t_done"], m + 1)
                for t2 in range(2):
                    for t in range(4):
                        last = A(z["t"].rearrange("p g (t c) -> p g t c", t=CH)[:, :, 4 * t2 + t, :],
                                 bank[4 + t2][:, t * P:t * P + P].rearrange("p (g c) -> p g c", g=GPT), ACT.Copy)
                last.then_inc(s5["t_sb"], 1)
                act.wait_ge(s5["v"], m + 1)
                for part in range(2):
                    for qh in range(2):
                        last = A(z["v"][part][:, 2 * qh:2 * qh + 2, :],
                                 bank[2 * part + qh][:, 0:2 * NJ].rearrange("p (q j) -> p q j", q=2), ACT.Copy)
                last.then_inc(s5["v_sb"], 1)
                act.wait_ge(s5["y"], m + 2)
                for qh in range(2):
                    for b in range(2):
                        last = A(z["y"].rearrange("p (q b) j -> p q b j", b=2)[:, 2 * qh:2 * qh + 2, b, :],
                                 bank[4 + 2 * qh + b][:, 0:2 * NJ].rearrange("p (q j) -> p q j", q=2), ACT.Copy)
                last.then_inc(s5["y_sb"], 1)
                act.wait_ge(s5["y_sb"], m + 1)
                for t in range(CH):
                    act.dma_start(s5_y[m, t].rearrange("(g c) j -> c g j", g=GPT),
                                  z["y"][t * G_CH:t * G_CH + G_CH]).then_inc(s5["y_stored"], 16)
                act.wait_ge(s5["y_stored"], (m + 1) * (16 * CH))
                act.dma_start(z["yh"].rearrange("p (s j) -> p s j", s=CH),
                              s5_y[m].rearrange("s c j -> c s j")).then_inc(s5["y_loaded"], 16)
                act.wait_ge(s5["skip"], m + 2)
                A(z["yh"], z["yh"], ACT.Gelu_apprx_tanh).then_inc(s5["gelu"], 1)
                act.wait_ge(s5["gelu"], m + 1)
                A(x_hi[:, m, :].rearrange("p (j s) -> p s j", s=CH), z["yh"].rearrange("p (s j) -> p s j", s=CH),
                  ACT.Copy).then_inc(s5["hi"], 1)

            act.sem_inc(s5["y"], 1)
            act.sem_inc(s5["skip"], 1)
            with act.Fori(0, KT) as m:
                s5_tile(m)

            gate, _f = ffn_views(carve)
            act.wait_ge(s5["lo"], KT)
            with act.Fori(0, 4) as i:
                for j in range(2):
                    for c, (a, n) in enumerate(CUTS):
                        at = 6 * i + 3 * j + c
                        act.wait_ge(group_done, GROUPS_BEFORE["glu"] + 2 * at + 2)
                        act.wait_ge(glu_mul, at + 2)
                        A(gate[(3 * j + c) % 2][:, 0:n], bank[2 * c + 1][:, 0:n], ACT.Sigmoid).then_inc(glu_gate, 1)
            act.wait_ge(glu_mul, 24 + 3)
            residual_block(3, resid[1], resid[2])
            ffn(1)
            residual_block(4, resid[2], outT)
            act.wait_ge(nm_stored[0], 16 * 8)
            act.wait_ge(nm_stored[1], 16 * 4)

        @block.vector
        def _(dve):
            V = nc.vector
            ch = Chain(dve, dve_chain_sem)
            mul, sub, add = ALU.mult, ALU.subtract, ALU.add

            def residual_block(r, pre_w, post_w):
                for c, m in norm_steps(r):
                    a, n = CUTS[c]
                    p, e = 3 * r + c, norm_event(r, c, m)
                    h, nb, rr = nv["h"][c % 2][:, :, 0:n], nv["nb"][:, :, 0:n], nv["rs"][e % 2][:, 0:n]
                    dve.wait_ge(nm_root, e + 1)
                    V.reciprocal(rr, rr).then_inc(nm_recip, 1)
                    dve.wait_ge(nm_recip, e + 1)
                    if m == 0:
                        for k in range(KT):
                            last = V.scalar_tensor_tensor(out=acc[:, k, a:a + n], in0=acc[:, k, a:a + n],
                                                          scalar=small[:, post_w + k:post_w + k + 1],
                                                          in1=rr, op0=mul, op1=mul)
                        ch(last)
                        ch.sync()
                        dve.wait_ge(nm_loaded[c % 2], 16 * (r + 1 if c == 1 else 2 * r + c // 2 + 1))
                        V.tensor_tensor(h, h, acc[:, :, a:a + n], add).then_inc(nm_resid, 1)
                    else:
                        for k in range(KT):
                            last = V.scalar_tensor_tensor(out=nb[:, k, :], in0=h[:, k, :],
                                                          scalar=small[:, pre_w + k:pre_w + k + 1],
                                                          in1=rr, op0=mul, op1=mul)
                        last.then_inc(nm_normed, 1)
                        dve.wait_ge(nm_high, p + 1)
                        V.tensor_tensor(x_lo[:, :, a:a + n], nb, x_hi[:, :, a:a + n].bitcast(F32), sub).then_inc(x_ready, 1)

            V.memset(sb_eps[:, 0:1], EPS).then_inc(eps_ready, 1)
            V.memset(sb_eps[:, 1:2], EPS * HD).then_inc(eps_ready, 1)
            V.memset(carve(18300, T_PAD - T), 0.0).then_inc(eps_ready, 1)
            for s_, k_ in ((act_f32, 2), (down_free, 4), (conv_done, 2), (dn["out"], 2), (sk["logw"], 2), (sk["o_lo"], 2),
                           (glu_mul, 3), (proj_out, 2)):
                for _i in range(k_):
                    dve.sem_inc(s_, 1)
            dve.wait_ge(params_loaded, 32)
            residual_block(0, MIX_PRE, None)

            rows = carve(0, T_ROWS)
            ga, gb, keep = carve(T_ROWS, T_ROWS), carve(2 * T_ROWS, T_ROWS), carve(3 * T_ROWS, T_ROWS)
            cb, ct, po = conv_views(carve)
            ch(V.memset(rows, 0.0))
            ch(V.memset(ga, 0.0))
            ch(V.memset(keep, 1.0))
            ch.sync()
            ch(V.memset(keep.rearrange("p (b t) -> p b t", t=P)[:, :, 0:1], 0.0))
            for i in range(2):
                ch(V.memset(cb[i][:, 0:3], 0.0))
            ch.sync()
            V.memset(gb, 0.0).then_inc(gate_dve, 1)
            dve.wait_ge(gate_act, 1)
            ch(V.tensor_scalar(rows[32:36, 0:T], rows[32:36, 0:T], 1.0, None, add))
            ch.sync()
            V.reciprocal(rows[32:36, 0:T], rows[32:36, 0:T]).then_inc(gate_dve, 1)
            ch(V.scalar_tensor_tensor(out=ga[0:4, 0:T], in0=ga[0:4, 0:T], scalar=0.0, in1=gb[0:4, 0:T], op0=ALU.max, op1=add))
            ch.sync()
            ch(V.tensor_scalar(ga[0:4, 0:T], ga[0:4, 0:T], gate_col[0:4, :], -1.0, mul, mul))
            ch.sync()
            V.tensor_tensor_scan(rows[0:4, :], keep[0:4, :], ga[0:4, :], 0.0, mul, add).then_inc(gate_dve, 1)

            with dve.Fori(0, 3) as i:
                ch.enter(i, 0, 12)
                for s in range(4):
                    u, par = 4 * i + s, s % 2
                    dve.wait_ge(group_free, 12 + 3 * u + 3)
                    dve.wait_ge(proj_out, u + 1)
                    ch(V.tensor_scalar(ct[par], cb[par][:, 3:3 + T], small[:, bass.ds(W_CONV + 4 * u + 3, 1)], None, mul))
                    for j in (2, 1, 0):
                        ch.sync()
                        ins = V.scalar_tensor_tensor(out=ct[par], in0=cb[par][:, j:j + T],
                                                     scalar=small[:, bass.ds(W_CONV + 4 * u + j, 1)], in1=ct[par],
                                                     op0=mul, op1=add)
                        if j:
                            ch(ins)
                    ins.then_inc(conv_done, 1)
            ch.leave(3)

            v = dn_views(carve)
            dve.wait_ge(cols_ready, 1)
            V.memset(v["state"], 0.0).then_inc(dn["state"], 1)

            def per_head(f):
                for h in range(HEADS):
                    last = f(h, slice(h * P, h * P + P))
                return last

            def dn_blocks(n0, sets, width=P):
                for s in range(sets):
                    n, B, w = n0 + s, bank[4 * s:4 * s + 4], v[s]
                    dve.wait_ge(dn["bcast"], n + 1)
                    g_col = lambda h: v["cols"][:, n, h:h + 1]
                    per_head(lambda h, hs: V.tensor_scalar(w["lt"][:, hs], B[2][:, hs], g_col(h), 0.0, sub, ALU.min))
                    V.tensor_tensor(w["ecol"], h4(B[2][:])[:, :, P - 1], v["cols"][:, n, 0:HEADS], sub
                                    ).then_inc(dn["expo"], 1)
                    dve.wait_ge(dn["scales"], n + 1)
                    ch(V.tensor_tensor(w["k"], w["k"], w["t1"], mul))
                    ch(V.tensor_tensor(w["v"], w["v"], B[3][:], mul))
                    ch(V.tensor_tensor(w["q"], w["q"], w["t2"], mul))
                    V.tensor_copy(w["gl"], h4(w["eg"])[:, :, P - 1])
                    ch.sync()
                    V.tensor_tensor(w["kb"], w["k"], B[3][:], mul).then_inc(dn["kq"], 1)
                    V.tensor_tensor(w["qd"], w["q"], w["eg"], mul).then_inc(dn["qd"], 1)
                for s in range(sets):
                    n, B, w = n0 + s, bank[4 * s:4 * s + 4], v[s]
                    dve.wait_ge(dn["decay"], n + 1)
                    ch(V.tensor_tensor(h4(w["lt"]), h4(w["lt"]), over_heads(incl), mul))
                    dve.wait_ge(dn["kk"], n + 1)
                    V.tensor_tensor(w["kb"], w["kb"], w["eg"], mul)
                    last = per_head(lambda h, hs: V.tensor_scalar(w["kd"][:, hs], B[3][:, hs], w["ecol"][:, h:h + 1],
                                                                  None, mul))
                    last.then_inc(dn["inputs_used"], 1)
                    ch.sync()
                    V.tensor_tensor(w["qk"], B[1][:], w["lt"], mul)
                    ch(V.tensor_tensor(w["lt"], B[0][:], w["lt"], mul))
                    ch.sync()
                    ch(V.tensor_tensor(h4(w["t1"]), h4(w["lt"]), over_heads(level(0)), mul))
                    ch.sync()
                    V.tensor_tensor(h4(w["u"]), over_heads(ident), h4(w["t1"]), sub).then_inc(dn["ident_minus"], 1)
                for lev in range(1, LEVELS):
                    at = n0 * (LEVELS - 1) + (lev - 1) * sets
                    for s in range(sets):
                        if lev == 1:
                            dve.wait_ge(dn["ident_minus"], n0 + s + 1)
                        V.tensor_tensor(h4(v[s]["t1"]), h4(v[s]["lt"]), over_heads(level(lev)), mul).then_inc(dn["masked"], 1)
                    for s in range(sets):
                        dve.wait_ge(dn["up"], at + s + 1)
                        V.tensor_tensor(v[s]["x"], v[s]["x"], bank[4 * s + 1][:], sub).then_inc(dn["x_new"], 1)
                for s in range(sets):
                    n, B, w = n0 + s, bank[4 * s:4 * s + 4], v[s]
                    dve.wait_ge(dn["ks"], n + 1)
                    V.tensor_tensor(w["t1"], w["vt"], B[0][:], sub).then_inc(dn["rhs"], 1)
                    dve.wait_ge(dn["o"], n + 1)
                    per_head(lambda h, hs: V.scalar_tensor_tensor(
                        out=v["state"][:, hs], in0=v["state"][:, hs], scalar=w["gl"][:, h:h + 1], in1=B[3][:, hs],
                        op0=mul, op1=add)).then_inc(dn["state"], 1)
                    dve.wait_ge(dn["o_scale"], n + 1)
                    per_head(lambda h, hs: V.tensor_scalar(w["x"][:, hs], B[2][:, hs], w["ss"][:, h:h + 1], None, mul)
                             ).then_inc(dn["o_norm"], 1)
                for s in range(sets):
                    n, B, w = n0 + s, bank[4 * s:4 * s + 4], v[s]
                    dve.wait_ge(dn["o_t"], n + 1)
                    dve.wait_ge(dn[f"z_loaded{s}"], 16 * (z_turn[0] + 1))
                    V.scalar_tensor_tensor(out=w["t1"], in0=B[0][:], scalar=small[:, W_ONORM:W_ONORM + 1], in1=w["z"],
                                           op0=mul, op1=mul).then_inc(dn["o_gated"], 1)
                    dve.wait_ge(dn["o_hi"], n + 1)
                    at = bass.ds(n * P, width)
                    V.tensor_tensor(x_lo[:, 0:HEADS, at], h4(w["t1"])[:, :, 0:width],
                                    x_hi[:, 0:HEADS, at].bitcast(F32), sub).then_inc(dn["out"], 1)

            z_turn = [0]
            with dve.Fori(0, (BLOCKS - 1) // 2) as i:
                z_turn[0] = i
                ch.enter(i, 0, 12)
                dn_blocks(2 * i, 2)
            ch.leave((BLOCKS - 1) // 2)
            z_turn[0] = (BLOCKS - 1) // 2
            dn_blocks(BLOCKS - 1, 1, TAIL)

            sv = sb_views(carve)

            def sb_mask(hd, i):
                nq, d0, nk = min(P, T - i * P), i * P, min(T, (i + 1) * P)
                e = sv["e"][i % 3]
                dve.wait_ge(sk["w"], hd * BLOCKS + i + 1)
                V.tensor_tensor(e[0:nq, d0:nk], e[0:nq, d0:nk], strict[0:nq, 0:nk - d0], mul).then_inc(sk["wm"], 1)

            def sb_low(hd, i):
                nq = min(P, T - i * P)
                dve.wait_ge(sk["o_hi"], hd * BLOCKS + i + 1)
                o = slice(i * P, i * P + nq)
                V.tensor_tensor(x_lo[:, HEADS + hd, o], bank[6 + i % 2][:, 0:nq], x_hi[:, HEADS + hd, o].bitcast(F32), sub
                                ).then_inc(sk["o_lo"], 1)

            with dve.Fori(0, HEADS) as hd:
                ch.enter(hd, 0, 4 * BLOCKS)
                for i in range(BLOCKS):
                    nq, nk = min(P, T - i * P), min(T, (i + 1) * P)
                    e, r, d0 = sv["e"][i % 3], sv["r"][i % 2], i * P
                    src = lambda a: bank[(2 * (i % 2) + a // 512) % 4]
                    pieces = [(a, min(512, nk - a)) for a in range(0, nk, 512)]
                    dve.wait_ge(sk["soft"], hd * BLOCKS + i + 1)
                    for a, m in pieces:
                        last = V.scalar_tensor_tensor(out=r[0:nq, a:a + m], in0=src(a)[0:nq, 0:m], scalar=0.0,
                                                      in1=e[0:nq, a:a + m], op0=ALU.max, op1=add)
                    ch(last)
                    ch.sync()
                    ch(V.tensor_tensor(r[0:nq, d0:nk], r[0:nq, d0:nk], strict[0:nq, 0:nk - d0], mul))
                    ch.sync()
                    rv = r[0:nq, nk - 1::-1] if nk == T else r[0:nq, 0:nk][:, ::-1]
                    ch(V.tensor_tensor_scan(rv, rv, rv, 0.0, add, ALU.max))
                    ch.sync()
                    for a, m in pieces:
                        last = V.tensor_tensor(e[0:nq, a:a + m], src(a)[0:nq, 0:m], r[0:nq, a:a + m], sub)
                    ch(last)
                    ch.sync()
                    V.tensor_scalar(e[0:nq, d0:nk], e[0:nq, d0:nk], 0.0, None, ALU.min).then_inc(sk["logw"], 1)
                    if i > 0:
                        sb_mask(hd, i - 1)
                    if i > 1:
                        sb_low(hd, i - 2)
                sb_mask(hd, BLOCKS - 1)
                sb_low(hd, BLOCKS - 2)
                sb_low(hd, BLOCKS - 1)
            ch.leave(HEADS)

            residual_block(1, FFN_PRE, MIX_POST)

            def ffn(layer):
                base = layer * PAIRS
                gate, f = ffn_views(carve)

                def pair(i, first):
                    for st in range(6):
                        a, n = CUTS[st % 3]
                        step = (base + i) * 6 + st
                        dve.wait_ge(silu_done, step + 1)
                        V.tensor_tensor(f[st % 2][:, 0:n], gate[st % 2][:, 0:n], bank[2 * (st % 2) + 1][:, 0:n], mul
                                        ).then_inc(act_f32, 1)
                        dve.wait_ge(act_high, step + 1)
                        V.tensor_tensor(act_lo[:, st // 3, a:a + n], f[st % 2][:, 0:n],
                                        act_hi[:, st // 3, a:a + n].bitcast(F32), sub).then_inc(act_ready, 1)
                    for c, (a, n) in enumerate(CUTS):
                        for m in range(KT):
                            dve.wait_ge(down_done, (base + i) * 24 + 8 * c + m + 2)
                            o, src = acc[:, m, a:a + n], bank[4 + m % 4][:, 0:n]
                            last = V.tensor_copy(o, src) if first else V.tensor_tensor(o, o, src, add)
                            last.then_inc(down_free, 1)

                pair(0, True)
                with dve.Fori(1, PAIRS) as i:
                    pair(i, False)

            ffn(0)
            residual_block(2, MIX_PRE + 8, FFN_POST)

            z = s5_views(carve)
            par = z["par"]
            lre, lim = par[:, S_LRE:S_LRE + 32], par[:, S_LIM:S_LIM + 32]
            tt = lambda o, a, b, op: ch(V.tensor_tensor(o, a, b, op))

            def cmul(ore, oim, are, aim, bre, bim, t0, t1, conj=False):
                ch.sync()
                tt(t0, aim, bim, mul)
                tt(t1, aim, bre, mul)
                tt(ore, are, bre, mul)
                tt(oim, are, bim, mul)
                ch.sync()
                tt(ore, ore, t0, add if conj else sub)
                tt(oim, oim, t1, sub if conj else add)
                ch.sync()

            dve.wait_ge(s5["act"], 1)
            tt(z["lr"], lre, z["dt"], mul)
            tt(z["ta"], lim, z["dt"], mul)
            ch.sync()
            ch(V.tensor_scalar(z["turns"], z["ta"], float(1 / (2 * np.pi)), None, mul))
            ch.sync()
            ch(V.tensor_copy(z["tb"], z["turns"]))
            ch.sync()
            for part in (TWO_PI_A, TWO_PI_B, TWO_PI_C):
                ch(V.scalar_tensor_tensor(out=z["ta"], in0=z["tb"], scalar=-part, in1=z["ta"], op0=mul, op1=add))
                ch.sync()
            V.tensor_scalar(z["ang"], z["ta"], 3.1415925, -3.1415925, ALU.min, ALU.max).then_inc(s5["angles"], 1)
            dve.wait_ge(s5["act"], 2)
            tt(z["ta"], z["half"], z["half"], mul)
            ch.sync()
            ch(V.tensor_scalar(z["cos"], z["ta"], -2.0, 1.0, mul, add))
            ch.sync()
            p_re, p_im = z["pw"]
            ch(V.memset(p_re[:, 0, :], 1.0))
            ch(V.memset(p_im[:, 0, :], 0.0))
            tt(p_re[:, 1, :], z["mag"], z["cos"], mul)
            tt(p_im[:, 1, :], z["mag"], z["sin"], mul)
            tt(z["ta"], lre, lre, mul)
            tt(z["tb"], lim, lim, mul)
            ch.sync()
            tt(z["den"], z["ta"], z["tb"], add)
            ch(V.tensor_scalar(z["are"], p_re[:, 1, :], -1.0, None, add))
            ch.sync()
            ch(V.reciprocal(z["den"], z["den"]))
            cmul(z["fre"], z["fim"], lre, lim, z["are"], p_im[:, 1, :], z["ta"], z["tb"], conj=True)
            tt(z["fre"], z["fre"], z["den"], mul)
            tt(z["fim"], z["fim"], z["den"], mul)
            ch.sync()
            wide = lambda x: x.rearrange("p (q c) -> p q c", c=1).to_broadcast([P, S_PAIRS, G_CH])
            b3 = lambda at: par[:, at:at + 512].rearrange("p (q c) -> p q c", c=G_CH)
            bre, bim, cre, cim = (b3(x) for x in (S_BRE, S_BIM, S_CRE, S_CIM))
            ch.sync()
            fre, fim = wide(z["fre"]), wide(z["fim"])
            t0, t1 = (x.rearrange("p (q c) -> p q c", c=G_CH) for x in z["tmp"])
            t2 = carve(0, S_PAIRS, G_CH)
            tt(t0, fim, bim, mul)
            tt(t1, fim, bre, mul)
            tt(t2, fre, bim, mul)
            ch.sync()
            tt(bre, fre, bre, mul)
            tt(bim, t2, t1, add)
            ch.sync()
            tt(bre, bre, t0, sub)
            sm = lambda x, n, w: x.rearrange("p (n w) -> p n w", w=w)[:, 0:n, :]
            for have in (1, 2, 4):
                o = slice(have + 1, 2 * have + 1)
                by = lambda p: p[:, have:have + 1, :].to_broadcast([P, have, S_PAIRS])
                cmul(p_re[:, o, :], p_im[:, o, :], by(p_re), by(p_im), p_re[:, 1:have + 1, :], p_im[:, 1:have + 1, :],
                     sm(z["tmp"][0], have, S_PAIRS), sm(z["tmp"][1], have, S_PAIRS))
            for part in range(2):
                for s in range(CH):
                    ch(V.tensor_copy(z["pr"][part][:, s, :], z["pw"][part][:, CH - 1 - s, :]))

            c_re, c_im = z["cos"], z["sin"]
            for _i in range(3):
                cmul(z["ta"], z["tb"], c_re, c_im, c_re, c_im, z["fre"], z["fim"])
                ch(V.tensor_copy(c_re, z["ta"]))
                ch(V.tensor_copy(c_im, z["tb"]))
                ch.sync()
            for tab, size in ((z["ph_b"], 16), (z["ph_a"], 9)):
                re, im = tab
                ch(V.memset(re[:, :, 0:1], 1.0))
                ch(V.memset(im[:, :, 0:1], 0.0))
                ch(V.tensor_copy(re[:, :, 1:2], c_re.rearrange("p (q o) -> p q o", o=1)))
                ch(V.tensor_copy(im[:, :, 1:2], c_im.rearrange("p (q o) -> p q o", o=1)))
                ch.sync()
                have = 1
                while have < size - 1:
                    more = min(have, size - 1 - have)
                    by = lambda p: p[:, :, have:have + 1].to_broadcast([P, S_PAIRS, more])
                    cmul(re[:, :, have + 1:have + 1 + more], im[:, :, have + 1:have + 1 + more], by(re), by(im),
                         re[:, :, 1:1 + more], im[:, :, 1:1 + more],
                         sm(z["tmp"][0], S_PAIRS, G_CH)[:, :, 0:more], sm(z["tmp"][1], S_PAIRS, G_CH)[:, :, 0:more])
                    have += more
                if size == 16:
                    cmul(z["ta"], z["tb"], re[:, :, 15], im[:, :, 15], c_re, c_im, z["fre"], z["fim"])
                    c_re, c_im = z["ta"], z["tb"]
            for part in range(2):
                ch(V.memset(z["x"][part][:, :, 0:1], 0.0))
            ch.sync()

            def s5_tile(m):
                qs = bass.ts(m, QP)
                w4 = [P, QP, CH, G_CH]
                pick = lambda p, lo: p[:, lo:lo + CH, qs]
                a_in = lambda p: pick(p, 0).rearrange("p s (q c) -> p q s c", c=1).to_broadcast(w4)
                a_out = lambda p: pick(p, 1).rearrange("p s (q c) -> p q s c", c=1).to_broadcast(w4)
                bc = lambda x: x[:, qs, :].rearrange("p q (s c) -> p q s c", s=1).to_broadcast(w4)
                v4 = lambda x: x.rearrange("p q (s c) -> p q s c", s=CH)
                t0, t1 = (carve(QP * P * i, QP, P) for i in range(2))
                cmul(v4(z["m"][0]), v4(z["m"][1]), a_in(z["pr"][0]), a_in(z["pr"][1]), bc(bre), bc(bim), v4(t0), v4(t1))
                ch(V.tensor_copy(z["cc"][0], cre[:, qs, :]))
                ch.sync()
                V.tensor_scalar(z["cc"][1], cim[:, qs, :], -1.0, None, mul).then_inc(s5["win"], 1)
                cmul(v4(z["wout"][0]), v4(z["wout"][1]), a_out(p_re), a_out(p_im), bc(cre), bc(cim), v4(t0), v4(t1))
                ch(V.tensor_scalar(z["wout"][1], z["wout"][1], -1.0, None, mul))
                w4 = [P, QP, 9, 16]
                pa = lambda p: p[:, qs, :].rearrange("p q (a o) -> p q a o", o=1).to_broadcast(w4)
                pb = lambda p: p[:, qs, :].rearrange("p q (o b) -> p q o b", o=1).to_broadcast(w4)
                o4 = lambda x: x.rearrange("p q (a b) -> p q a b", b=16)
                t0, t1 = (carve(QP * 144 * i, QP, 144) for i in range(2))
                ch.sync()
                cmul(o4(z["ph"][0]), o4(z["ph"][1]), pa(z["ph_a"][0]), pa(z["ph_a"][1]), pb(z["ph_b"][0]),
                     pb(z["ph_b"][1]), o4(t0), o4(t1))
                ch(V.tensor_copy(z["m8"], z["mag8"][:, qs].rearrange("p (q o) -> p q o", o=1).to_broadcast([P, QP, NJ])))
                ch.sync()
                ch(V.memset(z["m8"][:, :, 0:1], 0.0))
                dve.wait_ge(s5["v_sb"], m + 1)
                f_re, f_im = (x[:, :, 0:NJ] for x in z["ph"])
                r = z["rot"]
                ch.sync()
                cmul(r[0], r[1], f_re, f_im, z["v"][0], z["v"][1], r[2], r[3], conj=True)
                flat = lambda x: x.rearrange("p q j -> p (q j)")
                for part in range(2):
                    ch(V.tensor_tensor_scan(flat(z["v"][part]), flat(z["m8"]), flat(r[part]), 0.0, mul, add))
                ch.sync()
                x_re, x_im = (x[:, :, 1:NJ + 1] for x in z["x"])
                tt(r[2], f_im, z["v"][1], mul)
                tt(r[3], f_im, z["v"][0], mul)
                tt(x_re, f_re, z["v"][0], mul)
                tt(x_im, f_re, z["v"][1], mul)
                ch.sync()
                ch(V.tensor_tensor(x_re, x_re, r[2], sub))
                V.tensor_tensor(x_im, x_im, r[3], add).then_inc(s5["x"], 1)
                dve.wait_ge(s5["y_loaded"], (m + 1) * 16)
                dve.wait_ge(s5["h_loaded"], (m + 1) * 16)
                V.scalar_tensor_tensor(out=z["yh"], in0=z["h"], scalar=small[:, bass.ds(D_SKIP + m, 1)], in1=z["yh"],
                                       op0=mul, op1=add).then_inc(s5["skip"], 1)
                dve.wait_ge(s5["hi"], m + 1)
                dst = lambda x: x[:, m, :].rearrange("p (j s) -> p s j", s=CH)
                V.tensor_tensor(dst(x_lo), z["yh"].rearrange("p (s j) -> p s j", s=CH), dst(x_hi).bitcast(F32), sub
                                ).then_inc(s5["lo"], 1)
                dve.wait_ge(s5["lo"], m + 1)

            with dve.Fori(0, KT) as m:
                ch.enter(m, 0, S5_MARKS)
                s5_tile(m)
            ch.leave(KT)

            gate, _f = ffn_views(carve)
            with dve.Fori(0, 4) as i:
                for j in range(2):
                    for c, (a, n) in enumerate(CUTS):
                        dve.wait_ge(glu_gate, 6 * i + 3 * j + c + 1)
                        last = V.tensor_tensor(acc[:, 2 * i + j, a:a + n], bank[2 * c][:, 0:n],
                                               gate[(3 * j + c) % 2][:, 0:n], mul)
                        last.then_inc(glu_mul, 1)
            residual_block(3, FFN_PRE + 8, MIX_POST + 8)
            ffn(1)
            residual_block(4, None, FFN_POST + 8)


def kernel(**inputs):
    import concourse.bacc as bacc
    from concourse.bass_utils import run_bass_kernel_spmd

    f = {k: np.ascontiguousarray(v) for k, v in inputs.items()}
    assert all(v.dtype == np.float32 for v in f.values())

    def feature_major(x):
        return x.reshape(x.shape[0], -1, P).transpose(2, 1, 0)

    def slabs(w):
        return w.reshape(KT, P, -1, P).transpose(2, 1, 0, 3).reshape(-1, P, KT * P)

    def ffn_slabs(layer):
        gate, up = slabs(f["ffn_w_gate"][layer]), slabs(f["ffn_w_up"][layer])
        down = f["ffn_w_down"][layer].reshape(PAIRS, 2, P, 2, 512).transpose(0, 3, 2, 1, 4).reshape(PAIRS, 2, P, 1024)
        out = []
        for p in range(PAIRS):
            out += [gate[2 * p], up[2 * p], gate[2 * p + 1], up[2 * p + 1], down[p, 0], down[p, 1]]
        return np.stack(out)

    w_in = f["hyb_w_in"][0]
    da = HEADS * HD
    gates = np.zeros((D, P), np.float32)
    gates[:, 0:4] = w_in[:, 4 * da + 4:4 * da + 8]
    gates[:, 32:36] = w_in[:, 4 * da:4 * da + 4]
    glu = slabs(f["ssm_w_glu"][0])
    stream = np.concatenate([
        slabs(gates), slabs(w_in[:, :4 * da]), slabs(w_in[:, 4 * da + 8:]), slabs(f["hyb_w_out"][0]), ffn_slabs(0),
        slabs(f["ssm_w_in"][0]), np.stack([glu[:KT], glu[KT:]], axis=1).reshape(2 * KT, P, 1024), ffn_slabs(1)])
    assert stream.shape == (N_SLABS, P, 1024)

    small = np.zeros((P, N_SMALL), np.float32)
    for at, name in ((MIX_PRE, "norm_mix_pre"), (MIX_POST, "norm_mix_post"), (FFN_PRE, "norm_ffn_pre"),
                     (FFN_POST, "norm_ffn_post")):
        small[:, at:at + 16] = f[name].reshape(2 * KT, P).T
    small[:, W_CONV:W_CONV + 48] = f["hyb_conv_w"][0].reshape(4, 12, P).transpose(2, 1, 0).reshape(P, 48)
    small[:, W_ONORM] = f["dn_out_norm"][0]
    small[0:4, A_LOG] = f["dn_a_log"][0]
    small[0:4, DT_BIAS] = f["dn_dt_bias"][0]
    small[:, D_SKIP:D_SKIP + 8] = f["ssm_d"][0].reshape(KT, P).T

    const = np.zeros((P, N_CONST), np.float32)
    i, j = np.meshgrid(np.arange(P), np.arange(P))
    const[:, C_ID:C_ID + P] = const[:, C_SHIFT:C_SHIFT + P] = i == j
    const[:, C_ONES:C_ONES + P] = 1
    const[:, C_INCL:C_INCL + P] = i >= j
    const[:, C_STRICT:C_STRICT + P] = i < j
    for lev in range(LEVELS):
        b = 1 << lev
        const[:, C_LEVEL + P * lev:C_LEVEL + P * lev + P] = (i // (2 * b) == j // (2 * b)) & (i // b % 2 == 1) & (j // b % 2 == 0)
    for h in range(HEADS):
        const[h, C_SEL + h * P:C_SEL + h * P + P] = 1
        const[32 + h, C_SEL + (4 + h) * P:C_SEL + (5 + h) * P] = 1

    def pairs(x):
        return x.reshape((S_PAIRS, 2 * STATE) + x.shape[2:]).swapaxes(0, 1)

    s5 = np.concatenate([
        pairs(f["ssm_lambda_re"][0]), pairs(f["ssm_lambda_im"][0]),
        pairs(np.repeat(f["ssm_log_step"][0][:, None], STATE, axis=1)),
        pairs(f["ssm_b_re"][0]).reshape(P, -1), pairs(f["ssm_b_im"][0]).reshape(P, -1),
        pairs(f["ssm_c_re"][0].swapaxes(1, 2)).reshape(P, -1), pairs(f["ssm_c_im"][0].swapaxes(1, 2)).reshape(P, -1)],
        axis=1)
    assert s5.shape == (P, N_S5)

    arrays = {
        "xT": feature_major(np.concatenate([f["meta_tokens"], f["x"][0]])), "wstream": stream, "small_in": small,
        "const_in": const, "s5_in": s5}
    arrays = {k: np.ascontiguousarray(a) for k, a in arrays.items()}
    nc = bacc.Bacc("TRN2", target_bir_lowering=False, num_devices=1, dynamic_dma_scratch_size=1024)
    aps = [nc.dram_tensor(k, a.shape, F32, kind="ExternalInput").ap() for k, a in arrays.items()]
    out = nc.dram_tensor("outT", (P, KT, SEQ), F32, kind="ExternalOutput").ap()
    trunk(nc, *aps, out)
    r = run_bass_kernel_spmd(nc, [arrays], core_ids=[0])
    got = r.results[0]["outT"]
    return np.ascontiguousarray(got.transpose(2, 1, 0)).reshape(1, SEQ, D)
```

```python
from contextlib import ExitStack

import numpy as np

import concourse.bass as bass
from concourse import mybir

F32 = mybir.dt.float32
F32R = mybir.dt.float32r
I32 = mybir.dt.int32
ALU = mybir.AluOpType
ACT = mybir.ActivationFunctionType

P = 128
N_META, SEQ, D = 16, 1024, 1024
T = N_META + SEQ
KT = D // P
HEADS = 4
HD = 128
EPS = 1e-6
D_FF = 2816
PAIRS = D_FF // (2 * P)

CUTS = [(0, 352), (352, 344), (696, 344)]
HALF_CUTS = [(0, 176), (176, 176), (352, 172), (524, 172), (696, 172), (868, 172)]
CW = 352

BLOCKS = (T + P - 1) // P
TAIL = T - (BLOCKS - 1) * P
T_ROWS = BLOCKS * P
T_PAD = (BLOCKS + 1) * P

DQ, DK, DV, DZ, SQ, SK, SV = 0, 4, 8, 12, 16, 20, 24
N_PROJ = 28

G_CH, STATE, CH = 16, 64, 8
N_GROUPS = D // G_CH
S_PAIRS = N_GROUPS // 2
NJ = T // CH
QP = 4
GPT = 8

SLOTS = 6
STREAM = [
    ("gates", 1, [5]),
    ("in_proj", 7, [0, 1, 2, 3]),
    ("w_out", 2, [0, 1, 2, 3]),
    ("ffn0", PAIRS, [0, 1, 2, 3, 4, 5]),
    ("ssm_in", 2, [0, 1, 2, 3]),
    ("glu", 4, [0, 1, 2, 3]),
    ("ffn1", PAIRS, [0, 1, 2, 3, 4, 5]),
]
N_SLABS = sum(n * len(s) for _, n, s in STREAM)

(MIX_PRE, MIX_POST, FFN_PRE, FFN_POST), W_CONV, W_ONORM, A_LOG, DT_BIAS = (
    [0, 16, 32, 48], 64, 112, 113, 114)
N_SMALL = 115
C_ID, C_ONES, C_INCL, C_STRICT, C_SHIFT, C_LEVEL, C_SEL = [P * i for i in (0, 1, 2, 3, 4, 6, 13)]
N_CONST = P * 21
LEVELS = 7
S_LRE, S_LIM, S_LOG, S_BRE, S_BIM, S_CRE, S_CIM, S_D = 0, 32, 64, 96, 608, 1120, 1632, 2144
N_S5 = S_D + N_GROUPS

TWO_PI_A = 6.28125
TWO_PI_B = float(np.float32(0.00193500518798828125))
TWO_PI_C = float(2 * np.pi - TWO_PI_A - TWO_PI_B)


GROUPS_BEFORE = {"gates": 0, "in_proj": 6, "w_out": 90, "ssm_in": 114, "glu": 138}
WT_BEFORE = [sum((i + 4) // 4 for i in range(b)) for b in range(BLOCKS)]
WT_GROUPS = 3 + sum((i + 4) // 4 for i in range(BLOCKS))
GATE_DVE = 3
S5_MARKS = 37


NORM_ORDER = ((0, 0), (1, 0), (0, 1), (2, 0), (1, 1), (2, 1))


def norm_steps(r):
    return [(c, m) for c, m in NORM_ORDER if (r > 0 or m == 1) and (r < 4 or m == 0)]


def norm_event(r, c, m):
    if r == 0:
        return c
    return 3 + 6 * (r - 1) + (NORM_ORDER.index((c, m)) if r < 4 else c)


class Chain:

    def __init__(self, eng, sem):
        self.eng, self.sem, self.n, self.loop = eng, sem, 0, None

    def __call__(self, ins):
        ins.then_inc(self.sem, 1)
        self.n += 1
        return ins

    def sync(self):
        if self.loop is None:
            self.eng.wait_ge(self.sem, self.n)
        else:
            i, per = self.loop
            self.eng.wait_ge(self.sem, i * per + self.n)

    def enter(self, i, i0, per):
        self.loop, self.start = (i, per), self.n
        self.n -= i0 * per
        self.i0 = i0

    def leave(self, count):
        i, per = self.loop
        assert self.n + self.i0 * per - self.start == per, (self.n + self.i0 * per - self.start, per)
        self.loop, self.n = None, self.start + count * per


def norm_views(carve, at):
    return {"h": [carve(at + KT * CW * i, KT, CW) for i in range(2)], "nb": carve(at + 2 * KT * CW, KT, CW),
            "sq": carve(at + 3 * KT * CW, KT // 2, CW),
            "rs": [carve(at + 7 * KT * CW // 2 + CW * i, CW) for i in range(2)]}


def conv_views(carve):
    at = 4 * T_ROWS
    return ([carve(at + (T + 4) * i, T + 3) for i in range(2)],
            [carve(at + 2 * (T + 4) + T * i, T) for i in range(2)],
            [carve(at + 2 * (T + 4) + T * (2 + i), T) for i in range(2)])


def ffn_views(carve):
    at = KT * T
    return [carve(at + CW * i, CW) for i in range(2)], [carve(at + CW * (2 + i), CW) for i in range(2)]


def dn_views(carve):
    v = {"rows": carve(0, T_ROWS), "cols": carve(T_ROWS, BLOCKS, 64), "state": carve(1728, 512)}
    for s in range(2):
        at = 2240 + 7700 * s
        v[s] = {x: carve(at + 512 * i, 512) for i, x in enumerate(
            ("q", "k", "v", "z", "kb", "qd", "eg", "lt", "qk", "x", "u", "t1", "t2", "vt", "kd"))}
        for i, x in enumerate(("ss", "ecol", "gl")):
            v[s][x] = carve(at + 512 * 15 + 4 * i, 4)
    return v


def sb_views(carve):
    v = {x: carve(T * i, T) for i, x in enumerate("qkv")}
    v["vt"], v["wt"] = carve(3 * T, BLOCKS * P), carve(3 * T + BLOCKS * P, BLOCKS, P)
    at = 3 * T + 2 * BLOCKS * P
    v["e"] = [carve(at + T * i, T) for i in range(3)]
    v["r"] = [carve(at + T * (3 + i), T) for i in range(2)]
    return v


def s5_views(carve):
    z, at = {}, 0

    def put(name, *shape, n=1):
        nonlocal at
        z[name] = [carve(at + i * int(np.prod(shape)), *shape) for i in range(n)]
        at += n * int(np.prod(shape))
        if n == 1:
            z[name] = z[name][0]
    z["ut"] = [carve(T * i, T) for i in range(4)]
    at = 2 * T
    z["yh"], z["y"] = carve(0, T), carve(T, GPT, NJ)
    put("rot", QP, NJ, n=4)
    rot_at = at - 4 * QP * NJ
    z["t128"] = [carve(rot_at + QP * P * i, QP, P) for i in range(2)]
    z["t144"] = [carve(rot_at + QP * 144 * i, QP, 144) for i in range(2)]
    put("par", N_S5)
    for x in ("dt", "lr", "mag", "mag8", "ang", "sin", "half", "cos", "are", "aim", "den", "fre", "fim", "ta", "tb", "turns"):
        put(x, S_PAIRS)
    z["turns"] = z["turns"].bitcast(I32)
    put("pw", CH + 1, S_PAIRS, n=2)
    put("pr", CH, S_PAIRS, n=2)
    put("ph_b", S_PAIRS, 16, n=2)
    put("ph_a", S_PAIRS, 9, n=2)
    put("tmp", S_PAIRS * G_CH, n=2)
    end, at = at, at - 2 * S_PAIRS * G_CH
    put("cc", QP, G_CH, n=2)
    put("k", P)
    put("dd", GPT, G_CH)
    put("m8", QP, NJ)
    assert at <= end
    at = end
    put("ph", QP, 144, n=2)
    put("m", QP, P, n=2)
    put("win", QP, P, n=2)
    put("t", GPT, P)
    put("wout", QP, P, n=2)
    put("u", GPT, NJ)
    put("v", QP, NJ, n=2)
    put("x", QP, NJ + 1, n=2)
    return z


def stream_uses(name, key):
    n = 0
    for phase, count, slots in STREAM:
        if phase == name:
            return n
        n += count * sum(1 for s in slots if key(s))
    return n


def first_slab(name):
    return stream_uses(name, lambda s: True)


def slots_of(name):
    return next((n, s) for phase, n, s in STREAM if phase == name)


def trunk(nc, xT, wstream, small_in, const_in, s5_in, outT):
    with ExitStack() as ctx:
        def sb(name, shape, dt=F32):
            return ctx.enter_context(nc.sbuf_tensor(name, shape, dt))

        def sem(name):
            return ctx.enter_context(nc.semaphore(name))

        resid = [nc.dram_tensor(f"resid{i}", (P, KT, T), F32, kind="Internal").ap() for i in range(3)]
        proj = nc.dram_tensor("proj", (N_PROJ, P, T_PAD), F32, kind="Internal").ap()
        s5_u = nc.dram_tensor("s5_u", (KT, CH, P, NJ), F32, kind="Internal").ap()
        s5_y = nc.dram_tensor("s5_y", (KT, CH, P, NJ), F32, kind="Internal").ap()

        x_hi = sb("x_hi", [P, KT, T], F32R)
        x_lo = sb("x_lo", [P, KT, T], F32R)
        act_hi = sb("act_hi", [P, 2, T], F32R)
        act_lo = sb("act_lo", [P, 2, T], F32R)
        w_hi = sb("w_hi", [P, SLOTS, 1024], F32R)
        w_lo = sb("w_lo", [P, SLOTS, 1024], F32R)
        stage = sb("stage", [P, 2, 1024])
        small = sb("small", [P, N_SMALL])
        const = sb("const", [P, N_CONST])
        AREA = 19000
        area = sb("area", [P, AREA])

        def carve(at, *shape):
            n = int(np.prod(shape))
            assert at + n <= AREA, (at, n)
            v = area[:, at:at + n]
            if len(shape) == 2:
                v = v.rearrange("p (a b) -> p a b", a=shape[0])
            if len(shape) == 3:
                v = v.rearrange("p (a b c) -> p a b c", a=shape[0], b=shape[1])
            return v

        bank = [ctx.enter_context(nc.psum_tensor(f"bank{i}", [P, 512], F32)) for i in range(8)]

        ident = const[:, C_ID:C_ID + P]
        ones = const[:, C_ONES:C_ONES + P]
        incl = const[:, C_INCL:C_INCL + P]
        strict = const[:, C_STRICT:C_STRICT + P]

        def level(n):
            return const[:, C_LEVEL + P * n:C_LEVEL + P * n + P]

        def over_heads(m):
            return m.rearrange("p (a c) -> p a c", a=1).to_broadcast([P, HEADS, P])

        def h4(v):
            return v.rearrange("p (h c) -> p h c", h=HEADS)

        stage_loaded = [sem(f"stage_loaded{i}") for i in range(2)]
        split_done = sem("split_done")
        high_split = sem("high_split")

        params_loaded = sem("params_loaded")
        zeros_written = sem("zeros_written")
        x_ready = sem("x_ready")
        group_done = sem("group_done")
        group_free = sem("group_free")
        nm_loaded = [sem(f"nm_loaded{i}") for i in range(2)]
        nm_square = sem("nm_square")
        nm_root = sem("nm_root")
        nm_resid = sem("nm_resid")
        nm_normed = sem("nm_normed")
        nm_high = sem("nm_high")
        nm_sum = sem("nm_sum")
        nm_stored = [sem(f"nm_stored{i}") for i in range(2)]
        gate_dve = sem("gate_dve")
        gate_act = sem("gate_act")
        conv_done = sem("conv_done")
        glu_gate = sem("glu_gate")
        glu_mul = sem("glu_mul")
        proj_out = sem("proj_out")
        proj_stored = [sem(f"proj_stored{i}") for i in range(2)]
        cols_done = sem("cols_done")
        cols_ready = sem("cols_ready")
        dn = {k: sem("dn_" + k) for k in (
            "qkv_loaded0", "qkv_loaded1", "z_loaded0", "z_loaded1", "squares", "sums", "bcast", "scales",
            "kq", "qd", "vt", "expo", "kk", "decay", "ident_minus", "x_t", "x0", "masked", "p", "p_sb",
            "up", "x_new", "u_t", "u_sb", "ks", "rhs", "vn", "vn_sb", "o", "state", "o_scale",
            "o_norm", "o_t", "o_gated", "o_hi", "out")}
        sk = {k: sem("sb_" + k) for k in (
            "loaded", "tail_group", "z", "soft", "logw", "w", "wm", "w_t", "wt_sb",
            "o", "o_hi", "o_lo")}
        gu_done = sem("gu_done")
        silu_done = sem("silu_done")
        act_f32 = sem("act_f32")
        act_high = sem("act_high")
        act_ready = sem("act_ready")
        down_done = sem("down_done")
        down_free = sem("down_free")
        u_stored = [sem(f"u_stored{i}") for i in range(4)]
        s5 = {k: sem("s5_" + k) for k in (
            "angles", "t_done", "params", "act", "u_loaded", "win", "win_t", "win_sb",
            "k", "k_sb", "t_sb", "v", "v_sb", "x", "y", "y_sb", "y_stored", "y_loaded", "y_free",
            "gelu", "hi", "lo")}

        acc = carve(0, KT, T)
        A1 = KT * T

        nv = norm_views(carve, A1)

        def norm_bank(r, c, m):
            return bank[7 if r == 0 else c if r == 4 else 4 + NORM_ORDER.index((c, m)) % 4]

        acc_complete = {1: (group_free, 6 + GROUPS_BEFORE["ssm_in"]), 2: (down_free, 4 + 24 * PAIRS),
                        3: (glu_mul, 3 + 24), 4: (down_free, 4 + 48 * PAIRS)}
        sb_eps = sb("sb_eps", [P, 4])
        eps_ready = sem("eps_ready")
        gate_col = sb_eps[:, 2:3]
        act_chain_sem = sem("act_chain")
        dve_chain_sem = sem("dve_chain")

        def last_reader(name, i, slot):
            if name.startswith("ffn"):
                turn = int(name[3:]) * PAIRS + i
                return (gu_done, turn * 6 + slot // 2 + 5) if slot < 4 else (down_done, turn * 24 + 25)
            if name == "gates":
                return group_done, len(HALF_CUTS)
            if name == "ssm_in":
                return group_done, GROUPS_BEFORE[name] + i * 12 + 8 + slot + 1
            at = GROUPS_BEFORE[name] + i * 12
            return group_done, at + (6 * (slot // 2) + 6 if name == "glu" else 3 * slot + 3)

        def split_value(name, i, j):
            return first_slab(name) + i * len(slots_of(name)[1]) + j + 3

        block = ctx.enter_context(nc.Block())

        @block.sync
        def _(sp):
            z = s5_views(carve)

            def load_chunks(m):
                sp.wait_ge(s5["y"], m + 1)
                for t in range(CH):
                    sp.dma_start(z["u"][t * G_CH:t * G_CH + G_CH],
                                 s5_u[m, t].rearrange("(g c) j -> c g j", g=GPT)).then_inc(s5["u_loaded"], 16)

            def turn_outputs(m):
                sp.wait_ge(s5["y_sb"], m + 2)
                for t in range(CH):
                    sp.dma_start(s5_y[m, t].rearrange("(g c) j -> c g j", g=GPT),
                                 z["y"][t * G_CH:t * G_CH + G_CH]).then_inc(s5["y_stored"], 16)
                sp.wait_ge(s5["y_stored"], (m + 1) * (16 * CH))
                sp.sem_inc(s5["y_free"], 1)
                sp.wait_ge(s5["lo"], m + 1)
                sp.dma_start(z["yh"].rearrange("p (s j) -> p s j", s=CH),
                             s5_y[m].rearrange("s c j -> c s j")).then_inc(s5["y_loaded"], 16)

            def s5_transfers():
                sp.sem_inc(s5["y_free"], 1)
                for i in range(4):
                    sp.wait_ge(u_stored[i], 16 * 3)
                load_chunks(0)
                with sp.Fori(0, KT - 1) as m:
                    load_chunks(m + 1)
                    turn_outputs(m)
                turn_outputs(KT - 1)

            for name, count, slots in STREAM:
                base = first_slab(name)

                def load(i, name=name, slots=slots, base=base):
                    for j, slot in enumerate(slots):
                        n = base + i * len(slots) + j
                        sp.wait_ge(split_done, n + 1)
                        sp.dma_start(stage[:, slot % 2, :], wstream[n]).then_inc(stage_loaded[slot % 2], 16)
                if count == 1:
                    load(0)
                elif name == "glu":
                    load(0)
                    s5_transfers()
                    with sp.Fori(1, count) as i:
                        load(i)
                else:
                    with sp.Fori(0, count) as i:
                        load(i)

        @block.gpsimd
        def _(pool):
            for _i in range(2):
                pool.sem_inc(split_done, 1)
            last_of = {}

            def split(name, slots, i, before):
                for j, slot in enumerate(slots):
                    h = slot % 2
                    same = [s for s in slots if s % 2 == h]
                    use = stream_uses(name, lambda s: s % 2 == h) + i * len(same) + same.index(slot)
                    n = first_slab(name) + i * len(slots) + j
                    pool.wait_ge(stage_loaded[h], (use + 1) * 16)
                    if before is not None:
                        pool.wait_ge(*last_reader(before, i - 1, slot))
                    elif slot in last_of:
                        pool.wait_ge(*last_reader(*last_of[slot], slot))
                    per_block = lambda w: w.rearrange("p (k c) -> p k c", c=P)
                    pool.tensor_tensor(per_block(w_hi[:, slot, :]), per_block(stage[:, h, :]), all_ones, ALU.mult
                                       ).then_inc(high_split, 1)
                    pool.wait_ge(high_split, n + 1)
                    pool.tensor_tensor(w_lo[:, slot, :], stage[:, h, :], w_hi[:, slot, :].bitcast(F32),
                                       ALU.subtract).then_inc(split_done, 1)

            all_ones = ones.rearrange("p (a c) -> p a c", a=1).to_broadcast([P, KT, P])
            pool.wait_ge(params_loaded, 32)
            for name, count, slots in STREAM:
                split(name, slots, 0, None)
                if count == 2:
                    split(name, slots, 1, name)
                elif count > 2:
                    with pool.Fori(1, count) as i:
                        split(name, slots, i, name)
                for slot in slots:
                    last_of[slot] = (name, count - 1)

        @block.tensor
        def _(pe):
            mm = pe.matmul

            def gemm(out, slot, k, xk, cut, first, last, hi=x_hi, lo=x_lo):
                a, n = cut
                wk = slice(k * P, k * P + P)
                mm(out[:, 0:n], w_hi[:, slot, wk], hi[:, xk, a:a + n], start=first, stop=False)
                mm(out[:, 0:n], w_hi[:, slot, wk], lo[:, xk, a:a + n], start=False, stop=False)
                return mm(out[:, 0:n], w_lo[:, slot, wk], hi[:, xk, a:a + n], start=False, stop=last)

            def tile_groups(name, i, group0, cuts=CUTS, x_from=None):
                _, slots = slots_of(name)
                for j, slot in enumerate(slots):
                    pe.wait_ge(split_done, split_value(name, i, j))
                    for c, cut in enumerate(cuts):
                        g = group0 + (i * len(slots) + j) * len(cuts) + c
                        b = bank[(j * len(cuts) + c) % 6]
                        pe.wait_ge(group_free, g + 1)
                        if x_from is not None and j == 0:
                            pe.wait_ge(x_ready, x_from(c))
                        for k in range(KT):
                            last = gemm(b, slot, k, k, cut, k == 0, k == KT - 1)
                        last.then_inc(group_done, 1)

            def pair_groups(i):
                _, slots = slots_of("glu")
                for j in range(0, len(slots), 2):
                    pe.wait_ge(split_done, split_value("glu", i, j + 1))
                    for c, cut in enumerate(CUTS):
                        for v in range(2):
                            if v == 0:
                                pe.wait_ge(glu_mul, i * 6 + 3 * (j // 2) + c + 1)
                            for k in range(KT):
                                last = gemm(bank[2 * c + v], slots[j + v], k, k, cut, k == 0, k == KT - 1)
                            last.then_inc(group_done, 1)

            def norm_sums(r, first_piece=None):
                for c, m in norm_steps(r):
                    if first_piece is not None and (c, m) == NORM_ORDER[5]:
                        first_piece()
                    a, n = CUTS[c]
                    e = norm_event(r, c, m)
                    for k in range(KT):
                        if k % 4 == 0:
                            pe.wait_ge(nm_square, 2 * e + k // 4 + 1)
                        last = mm(norm_bank(r, c, m)[:, 0:n], ones, nv["sq"][:, k % 4, 0:n], start=(k == 0),
                                  stop=(k == KT - 1))
                        if k % 4 == 3:
                            last.then_inc(nm_sum, 1)

            def ffn(layer, r):
                name = f"ffn{layer}"
                base = layer * PAIRS

                def hidden(i, c, tiles=(0, 1)):
                    for f in tiles:
                        pe.wait_ge(split_done, split_value(name, i, 2 * f + 1))
                        step = (base + i) * 6 + 2 * c + f
                        pe.wait_ge(act_f32, step + 1)
                        for s in (2 * f, 2 * f + 1):
                            for k in range(KT):
                                last = gemm(bank[s], s, k, k, CUTS[c], k == 0, k == KT - 1)
                        last.then_inc(gu_done, 1)

                def down(i):
                    pe.wait_ge(split_done, split_value(name, i, 5))
                    for c, cut in enumerate(CUTS):
                        pe.wait_ge(act_ready, (base + i) * 6 + 2 * c + 2)
                        for m in range(KT):
                            pe.wait_ge(down_free, (base + i) * 24 + c * 8 + m + 1)
                            b = bank[4 + m % 4]
                            slot = 4 + m // 4
                            for kk in range(2):
                                last = gemm(b, slot, kk * 4 + m % 4, kk, cut, kk == 0, kk == 1, act_hi, act_lo)
                            last.then_inc(down_done, 1)

                def first_hidden(c, tiles=(0, 1)):
                    pe.wait_ge(x_ready, 3 * r + c + 1)
                    hidden(0, c, tiles)

                norm_sums(r, lambda: first_hidden(0, (0,)))
                first_hidden(0, (1,))
                first_hidden(1)
                first_hidden(2)
                down(0)
                with pe.Fori(1, PAIRS) as i:
                    for c in range(len(CUTS)):
                        hidden(i, c)
                    down(i)

            for s_, k_ in ((sk["wt_sb"], 2), (sk["o"], 2), (sk["z"], 1)):
                for _i in range(k_):
                    pe.sem_inc(s_, 1)
            pe.wait_ge(params_loaded, 32)

            norm_sums(0)
            tile_groups("gates", 0, 0, HALF_CUTS, x_from=lambda c: c // 2 + 1)
            with pe.Fori(0, 7) as i:
                tile_groups("in_proj", i, 6)

            rows = carve(0, T_ROWS)
            pe.wait_ge(gate_dve, GATE_DVE)
            for n in range(BLOCKS):
                last = pe.transpose(bank[6 + n // 8][:, n % 8 * 64:n % 8 * 64 + 64], rows[0:64, n * P:n * P + P],
                                    ident[0:64, 0:64])
            last.then_inc(cols_done, 1)

            v = dn_views(carve)

            def dn_parallel(n, s):
                B = bank[4 * s:4 * s + 4]
                q, k, w, kb = (v[s][x] for x in ("q", "k", "v", "kb"))
                pe.wait_ge(dn["squares"], n + 1)
                pe.wait_ge(dn["out"], n + 1)
                mm(B[0][:], ones, v[s]["t1"], start=True, stop=True)
                mm(B[1][:], ones, v[s]["t2"], start=True, stop=True).then_inc(dn["sums"], 1)

            def dn_broadcast(n, s):
                B = bank[4 * s:4 * s + 4]
                for h in range(HEADS):
                    hs = slice(h * P, h * P + P)
                    sel_g = const[0:64, C_SEL + h * P:C_SEL + h * P + P]
                    sel_b = const[0:64, C_SEL + (4 + h) * P:C_SEL + (5 + h) * P]
                    mm(B[2][:, hs], sel_g, rows[0:64, bass.ts(n, P)], start=True, stop=True)
                    last = mm(B[3][:, hs], sel_b, rows[0:64, bass.ts(n, P)], start=True, stop=True)
                last.then_inc(dn["bcast"], 1)

            def dn_products(n, s):
                B = bank[4 * s:4 * s + 4]
                q, k, w, kb = (v[s][x] for x in ("q", "k", "v", "kb"))
                pe.wait_ge(dn["kq"], n + 1)
                pe.wait_ge(dn["scales"], n + 1)
                for h in range(HEADS):
                    hs = slice(h * P, h * P + P)
                    mm(B[0][:, hs], k[:, hs], kb[:, hs], start=True, stop=True)
                    mm(B[1][:, hs], k[:, hs], q[:, hs], start=True, stop=True)
                for h in range(HEADS):
                    hs = slice(h * P, h * P + P)
                    pe.transpose(B[3][:, hs], k[:, hs], ident)
                    last = pe.transpose(B[2][:, hs], w[:, hs], ident)
                last.then_inc(dn["kk"], 1)

            def dn_first(n, s):
                B = bank[4 * s:4 * s + 4]
                pe.wait_ge(dn["ident_minus"], n + 1)
                pe.wait_ge(dn["vt"], n + 1)
                for h in range(HEADS):
                    hs = slice(h * P, h * P + P)
                    last = pe.transpose(B[2][:, hs], v[s]["u"][:, hs], ident)
                last.then_inc(dn["x_t"], 1)

            def dn_level_p(n, s, at):
                B = bank[4 * s:4 * s + 4]
                pe.wait_ge(dn["masked"], at + 1)
                if s is not None:
                    pe.wait_ge(dn["x0"], n + 1)
                for h in range(HEADS):
                    hs = slice(h * P, h * P + P)
                    last = mm(B[0][:, hs], v[s]["t1"][:, hs], v[s]["x"][:, hs], start=True, stop=True)
                last.then_inc(dn["p"], 1)

            def dn_level_up(n, s, at):
                B = bank[4 * s:4 * s + 4]
                pe.wait_ge(dn["p_sb"], at + 1)
                for h in range(HEADS):
                    hs = slice(h * P, h * P + P)
                    last = mm(B[1][:, hs], v[s]["u"][:, hs], v[s]["t2"][:, hs], start=True, stop=True)
                last.then_inc(dn["up"], 1)

            def dn_level_t(n, s, at):
                B = bank[4 * s:4 * s + 4]
                pe.wait_ge(dn["x_new"], at + 1)
                for h in range(HEADS):
                    hs = slice(h * P, h * P + P)
                    last = pe.transpose(B[2][:, hs], v[s]["x"][:, hs], ident)
                last.then_inc(dn["u_t"], 1)

            def dn_state(n, s, lvl):
                B = bank[4 * s:4 * s + 4]
                pe.wait_ge(dn["state"], n + 1)
                pe.wait_ge(dn["u_sb"], lvl)
                for h in range(HEADS):
                    hs = slice(h * P, h * P + P)
                    last = mm(B[0][:, hs], v[s]["kb"][:, hs], v["state"][:, hs], start=True, stop=True)
                last.then_inc(dn["ks"], 1)
                pe.wait_ge(dn["rhs"], n + 1)
                for h in range(HEADS):
                    hs = slice(h * P, h * P + P)
                    last = mm(B[1][:, hs], v[s]["u"][:, hs], v[s]["t1"][:, hs], start=True, stop=True)
                last.then_inc(dn["vn"], 1)
                pe.wait_ge(dn["vn_sb"], n + 1)
                for h in range(HEADS):
                    hs = slice(h * P, h * P + P)
                    mm(B[2][:, hs], v[s]["qd"][:, hs], v["state"][:, hs], start=True, stop=False)
                    mm(B[2][:, hs], v[s]["qk"][:, hs], v[s]["t2"][:, hs], start=False, stop=True)
                for h in range(HEADS):
                    hs = slice(h * P, h * P + P)
                    last = mm(B[3][:, hs], v[s]["kd"][:, hs], v[s]["t2"][:, hs], start=True, stop=True)
                last.then_inc(dn["o"], 1)

            def dn_out(n, s):
                B = bank[4 * s:4 * s + 4]
                pe.wait_ge(dn["o_norm"], n + 1)
                for h in range(HEADS):
                    hs = slice(h * P, h * P + P)
                    last = pe.transpose(B[0][:, hs], v[s]["x"][:, hs], ident)
                last.then_inc(dn["o_t"], 1)

            def dn_blocks(n0, sets, following):
                for s in range(sets):
                    dn_parallel(n0 + s, s)
                for s in range(sets):
                    dn_products(n0 + s, s)
                for s in range(sets):
                    dn_first(n0 + s, s)
                for lev in range(1, LEVELS):
                    at = n0 * (LEVELS - 1) + (lev - 1) * sets
                    for s in range(sets):
                        dn_level_p(n0 + s, s, at + s)
                    for s in range(sets):
                        dn_level_up(n0 + s, s, at + s)
                    for s in range(sets):
                        dn_level_t(n0 + s, s, at + s)
                for s in range(sets):
                    dn_state(n0 + s, s, (n0 + sets) * (LEVELS - 1))
                for s in range(sets):
                    dn_out(n0 + s, s)
                    if s < following:
                        dn_broadcast(n0 + 2 + s, s)

            pe.wait_ge(cols_ready, 1)
            for s in range(2):
                dn_broadcast(s, s)
            pairs = (BLOCKS - 1) // 2
            with pe.Fori(0, pairs - 1) as i:
                dn_blocks(2 * i, 2, 2)
            dn_blocks(2 * pairs - 2, 2, 1)
            dn_blocks(BLOCKS - 1, 1, 0)

            sv = sb_views(carve)
            pe.wait_ge(dn["out"], BLOCKS + 2)

            def sb_head(hd):
                w0 = hd * WT_GROUPS
                pe.wait_ge(sk["loaded"], 48 * (hd + 1))
                for g in range(3):
                    js = range(4 * g, min(4 * g + 4, BLOCKS))
                    pe.wait_ge(sk["wt_sb"], w0 + g + 1)
                    for j in js:
                        n = min(P, T - j * P)
                        last = pe.transpose(bank[4 + g % 2][0:n, j % 4 * P:j % 4 * P + P],
                                            sv["v"][:, j * P:j * P + n], ident)
                    last.then_inc(sk["w_t"], 1)

                sb_scores(hd, 0)
                for i in range(BLOCKS + 2):
                    if i > 1:
                        sb_turn(hd, i - 2, w0)
                    if i + 1 < BLOCKS - 1:
                        sb_scores(hd, i + 1)
                    if i > 1:
                        sb_out(hd, i - 2, w0)
                    if i + 1 == BLOCKS - 1:
                        sb_scores(hd, i + 1)

            def sb_scores(hd, i):
                nq, nk = min(P, T - i * P), min(T, (i + 1) * P)
                pe.wait_ge(sk["logw"], hd * BLOCKS + i + (1 if 0 < i < BLOCKS - 1 else 2))
                for a in range(0, nk, 512):
                    m = min(512, nk - a)
                    last = mm(bank[(2 * (i % 2) + a // 512) % 4][0:nq, 0:m], sv["q"][:, i * P:i * P + nq],
                              sv["k"][:, a:a + m], start=True, stop=True)
                last.then_inc(sk["z"], 1)

            def sb_turn(hd, i, w0):
                nq, nk = min(P, T - i * P), min(T, (i + 1) * P)
                pe.wait_ge(sk["wm"], hd * BLOCKS + i + 1)
                groups = [range(a, min(a + 4, i + 1)) for a in range(0, i + 1, 4)]
                base = w0 + 3 + WT_BEFORE[i]
                for gi, js in enumerate(groups):
                    g = base + gi
                    pe.wait_ge(sk["wt_sb"], g + 1)
                    if i == BLOCKS - 1:
                        pe.sem_inc(sk["tail_group"], 1)
                    for j in js:
                        n = min(P, T - j * P)
                        last = pe.transpose(bank[4 + (3 + WT_BEFORE[i] + gi) % 2][0:n, j % 4 * P:j % 4 * P + nq],
                                            sv["e"][i % 3][0:nq, j * P:j * P + n], ident[0:nq, 0:nq])
                    last.then_inc(sk["w_t"], 1)

            def sb_out(hd, i, w0):
                nq = min(P, T - i * P)
                pe.wait_ge(sk["wt_sb"], w0 + 3 + WT_BEFORE[i] + i // 4 + 3)
                pe.wait_ge(sk["o_lo"], hd * BLOCKS + i + (1 if i > 0 else 2))
                for j in range(i + 1):
                    n = min(P, T - j * P)
                    last = mm(bank[6 + i % 2][:, 0:nq], sv["vt"][0:n, j * P:j * P + P], sv["wt"][0:n, j, 0:nq],
                              start=(j == 0), stop=(j == i))
                last.then_inc(sk["o"], 1)

            with pe.Fori(0, HEADS) as hd:
                sb_head(hd)

            pe.wait_ge(sk["o_lo"], HEADS * BLOCKS + 2)
            with pe.Fori(0, 2) as i:
                tile_groups("w_out", i, GROUPS_BEFORE["w_out"])
            ffn(0, 1)

            def ssm_piece(i, c, tiles=range(4)):
                for j in tiles:
                    pe.wait_ge(split_done, split_value("ssm_in", i, j))
                    g = GROUPS_BEFORE["ssm_in"] + 12 * i + 4 * c + j
                    pe.wait_ge(group_free, g + 1)
                    for k in range(KT):
                        last = gemm(bank[(4 * c + j) % 6], j, k, k, CUTS[c], k == 0, k == KT - 1)
                    last.then_inc(group_done, 1)

            def first_piece(c, tiles=range(4)):
                pe.wait_ge(x_ready, 6 + c + 1)
                ssm_piece(0, c, tiles)

            norm_sums(2, lambda: first_piece(0, (0, 1)))
            first_piece(0, (2, 3))
            pe.wait_ge(nm_root, norm_event(2, 2, 1) + 1)
            first_piece(1)
            first_piece(2)
            for c in range(len(CUTS)):
                ssm_piece(1, c)

            z = s5_views(carve)

            def s5_tile(m):
                pe.wait_ge(s5["win"], m + 1)
                for part in range(2):
                    for q in range(QP):
                        last = pe.transpose(bank[part][:, q * P:q * P + P], z["m"][part][:, q, :], ident)
                last.then_inc(s5["win_t"], 1)
                for q in range(QP):
                    for b in range(2):
                        r = slice(STATE * b, STATE * b + STATE)
                        o = bank[2 + b][:, q * G_CH:q * G_CH + G_CH]
                        mm(o, z["m"][0][r, q, :], z["cc"][0][r, q, :],
                           start=True, stop=False)
                        last = mm(o, z["m"][1][r, q, :], z["cc"][1][r, q, :], start=False, stop=True)
                last.then_inc(s5["k"], 1)
                pe.wait_ge(s5["k_sb"], m + 1)
                pe.wait_ge(s5["y_sb"], m + 1)
                for t in range(CH):
                    off = C_SHIFT + G_CH * (CH - 1 - t)
                    last = mm(bank[4 + t // 4][:, t % 4 * P:t % 4 * P + P], const[:, off:off + P], z["k"],
                              start=True, stop=True)
                last.then_inc(s5["t_done"], 1)
                pe.wait_ge(s5["win_sb"], m + 1)
                pe.wait_ge(s5["u_loaded"], (m + 1) * (16 * CH))
                for part in range(2):
                    for q in range(QP):
                        for b in range(2):
                            r = slice(STATE * b, STATE * b + STATE)
                            o = bank[2 * part + q // 2][r, q % 2 * NJ:q % 2 * NJ + NJ]
                            last = mm(o, z["win"][part][:, q, r], z["u"][:, 2 * q + b, :], start=True, stop=True)
                last.then_inc(s5["v"], 1)
                pe.wait_ge(s5["t_sb"], m + 1)
                pe.wait_ge(s5["x"], m + 1)
                for q in range(QP):
                    for b in range(2):
                        r = slice(STATE * b, STATE * b + STATE)
                        o = bank[4 + 2 * (q // 2) + b][:, q % 2 * NJ:q % 2 * NJ + NJ]
                        mm(o, z["t"][:, 2 * q + b, :], z["u"][:, 2 * q + b, :], start=True, stop=False)
                        mm(o, z["wout"][0][r, q, :], z["x"][0][r, q, 0:NJ], start=False, stop=False)
                        last = mm(o, z["wout"][1][r, q, :], z["x"][1][r, q, 0:NJ], start=False, stop=True)
                last.then_inc(s5["y"], 1)

            pe.wait_ge(group_free, 6 + GROUPS_BEFORE["glu"])
            with pe.Fori(0, KT) as m:
                s5_tile(m)
            pe.wait_ge(s5["lo"], KT + 1)
            with pe.Fori(0, 4) as i:
                pair_groups(i)
            ffn(1, 3)
            norm_sums(4)

        @block.scalar
        def _(act):
            A = nc.scalar.activation
            eps_col = sb_eps[:, 0:1]
            ch = Chain(act, act_chain_sem)

            def residual_block(r, src, dst):
                def load(c):
                    a, n = CUTS[c]
                    p = 3 * r + c
                    if c >= 2:
                        act.wait_ge(*([nm_normed, p - 1] if r < 4 else [nm_resid, p - 1 - 3]))
                        if r > 0:
                            act.wait_ge(nm_stored[0], 16 * (2 * (r - 1) + 1))
                    act.dma_start(nv["h"][c % 2][:, :, 0:n], src[:, :, a:a + n]).then_inc(nm_loaded[c % 2], 16)

                def square(c, m):
                    a, n = CUTS[c]
                    if r == 0:
                        act.wait_ge(nm_loaded[c % 2], 16 * (c // 2 + 1))
                    e = norm_event(r, c, m)
                    x = nv["h"][c % 2][:, :, 0:n] if m else acc[:, :, a:a + n]
                    for half in range(2):
                        if e + half:
                            act.wait_ge(nm_sum, 2 * e + half)
                        A(nv["sq"][:, :, 0:n], x[:, 4 * half:4 * half + 4], ACT.Square).then_inc(nm_square, 1)

                def root(c, m):
                    n = CUTS[c][1]
                    e = norm_event(r, c, m)
                    act.wait_ge(nm_sum, 2 * e + 2)
                    if r > 0:
                        at = norm_steps(r).index((c, m))
                        if at >= 2:
                            c2, m2 = norm_steps(r)[at - 2]
                            act.wait_ge(*((nm_normed, 3 * r + c2 + 1) if m2 else (nm_resid, 3 * (r - 1) + c2 + 1)))
                    elif c == 2:
                        act.wait_ge(nm_normed, 1)
                    A(nv["rs"][e % 2][:, 0:n], norm_bank(r, c, m)[:, 0:n], ACT.Sqrt, scale=1.0 / D, bias=eps_col
                      ).then_inc(nm_root, 1)

                def store(c):
                    a, n = CUTS[c]
                    act.wait_ge(nm_resid, 3 * (r - 1) + c + 1)
                    skip = N_META if (r == 4 and c == 0) else 0
                    o = a - N_META if r == 4 else a
                    act.dma_start(dst[:, :, o + skip:o + n], nv["h"][c % 2][:, :, skip:n]).then_inc(nm_stored[c % 2], 16)

                def high(c):
                    a, n = CUTS[c]
                    act.wait_ge(nm_normed, 3 * r + c + 1)
                    A(x_hi[:, :, a:a + n], nv["nb"][:, :, 0:n], ACT.Copy).then_inc(nm_high, 1)

                load(0)
                load(1)
                if r == 0:
                    square(0, 1)
                    root(0, 1)
                    square(1, 1)
                    high(0)
                    root(1, 1)
                    load(2)
                    high(1)
                    square(2, 1)
                    root(2, 1)
                    high(2)
                    return
                act.wait_ge(*acc_complete[r])
                square(0, 0)
                root(0, 0)
                square(1, 0)
                if r == 4:
                    root(1, 0)
                    square(2, 0)
                    store(0)
                    load(2)
                    root(2, 0)
                    store(1)
                    store(2)
                    return
                root(1, 0)
                store(0)
                square(0, 1)
                root(0, 1)
                square(2, 0)
                root(2, 0)
                store(1)
                high(0)
                load(2)
                square(1, 1)
                root(1, 1)
                store(2)
                square(2, 1)
                high(1)
                root(2, 1)
                high(2)

            act.dma_start(small[:], small_in).then_inc(params_loaded, 16)
            act.dma_start(const[:], const_in).then_inc(params_loaded, 16)
            act.wait_ge(eps_ready, 3)
            zeros = carve(18300, T_PAD - T)
            for g in range(4):
                act.dma_start(proj[7 * g:7 * g + 7, :, T:T_PAD].rearrange("m p t -> p m t"),
                              zeros.rearrange("p (a t) -> p a t", a=1).to_broadcast([P, 7, T_PAD - T])
                              ).then_inc(zeros_written, 16)
            for _i in range(6):
                act.sem_inc(group_free, 1)
            for i in range(2):
                act.sem_inc(proj_stored[i], 16)
            for i in range(4):
                act.sem_inc(u_stored[i], 16)
            act.wait_ge(params_loaded, 32)
            residual_block(0, xT, None)

            rows = carve(0, T_ROWS)
            ga, gb = carve(T_ROWS, T_ROWS), carve(2 * T_ROWS, T_ROWS)
            act.wait_ge(nm_normed, 3)
            ch(A(gate_col[0:4, :], small[0:4, A_LOG:A_LOG + 1], ACT.Exp))
            act.wait_ge(gate_dve, 1)
            for c, (a, n) in enumerate(HALF_CUTS):
                act.wait_ge(group_done, c + 1)
                A(rows[32:36, a:a + n], bank[c][32:36, 0:n], ACT.Exp, scale=-1.0)
                A(ga[0:4, a:a + n], bank[c][0:4, 0:n], ACT.Identity, bias=small[0:4, DT_BIAS:DT_BIAS + 1]
                  ).then_inc(group_free, 1)
            act.wait_ge(group_free, 6 + 6)
            ch(A(gb[0:4, 0:T], ga[0:4, 0:T], ACT.Abs))
            ch.sync()
            ch(A(gb[0:4, 0:T], gb[0:4, 0:T], ACT.Exp, scale=-1.0))
            ch.sync()
            A(gb[0:4, 0:T], gb[0:4, 0:T], ACT.Ln, bias=1.0).then_inc(gate_act, 1)

            cb, ct, po = conv_views(carve)

            def proj_store(u, s):
                act.dma_start(proj[u][:, 0:T], po[s % 2]).then_inc(proj_stored[s % 2], 16)

            def conv_tiles(i):
                for s in range(4):
                    u = 4 * i + s
                    par = s % 2
                    act.wait_ge(conv_done, u + 1)
                    for c, (a, n) in enumerate(CUTS):
                        act.wait_ge(group_done, 6 + 3 * u + c + 1)
                        A(cb[par][:, 3 + a:3 + a + n], bank[(3 * s + c) % 6][:, 0:n], ACT.Copy).then_inc(group_free, 1)
                    act.wait_ge(conv_done, u + 3)
                    act.wait_ge(proj_stored[par], (2 * i + s // 2 + 1) * 16)
                    A(po[par], ct[par], ACT.Silu).then_inc(proj_out, 1)
                    act.wait_ge(proj_out, u + 3)
                    proj_store(u, s)

            def plain_tiles(i, func, scale=1.0):
                for s in range(4):
                    u = 4 * i + s
                    par = s % 2
                    act.wait_ge(proj_stored[par], (2 * i + s // 2 + 1) * 16)
                    for c, (a, n) in enumerate(CUTS):
                        act.wait_ge(group_done, 6 + 3 * u + c + 1)
                        last = A(po[par][:, a:a + n], bank[(3 * s + c) % 6][:, 0:n], func, scale=scale)
                        last.then_inc(group_free, 1)
                    act.wait_ge(group_free, 6 + 6 + 3 * u + 3)
                    proj_store(u, s)

            with act.Fori(0, 3) as i:
                conv_tiles(i)
            plain_tiles(3, ACT.Silu)
            plain_tiles(4, ACT.Copy, HD ** -0.5)
            with act.Fori(5, 7) as i:
                plain_tiles(i, ACT.Copy)

            v = dn_views(carve)
            nc.scalar.preload_act_table_set("natural_log_exp_and_others")
            for i in range(2):
                act.wait_ge(proj_stored[i], 16 * 15)
            act.wait_ge(zeros_written, 64)
            act.wait_ge(cols_done, 1)
            A(v["cols"][:, 0:8, :].rearrange("p a b -> p (a b)"), bank[6][:], ACT.Copy)
            A(v["cols"][:, 8, :], bank[7][:, 0:64], ACT.Copy).then_inc(cols_ready, 1)

            def dn_load(n, s, z):
                for m, x in ([(DZ, "z")] if z else [(DQ, "q"), (DK, "k"), (DV, "v")]):
                    act.dma_start(h4(v[s][x]), proj[m:m + 4, :, bass.ts(n, P)].rearrange("m p t -> p m t")
                                  ).then_inc(dn[("z" if z else "qkv") + f"_loaded{s}"], 16)

            act.wait_ge(gate_dve, GATE_DVE)
            for s in range(2):
                dn_load(s, s, False)
                dn_load(s, s, True)

            def dn_act_blocks(n0, i, sets, width=P):
                for s in range(sets):
                    act.wait_ge(dn[f"qkv_loaded{s}"], 48 * (i + 1))
                    act.wait_ge(dn["out"], n0 + s + 1)
                    A(v[s]["t1"], v[s]["k"], ACT.Square)
                    A(v[s]["t2"], v[s]["q"], ACT.Square).then_inc(dn["squares"], 1)
                for s in range(sets):
                    n, B = n0 + s, bank[4 * s:4 * s + 4]
                    act.wait_ge(dn["sums"], n + 1)
                    A(v[s]["t1"], B[0][:], ACT.Ln, bias=eps_col)
                    ch(A(v[s]["t2"], B[1][:], ACT.Ln, scale=float(HD), bias=sb_eps[:, 1:2]))
                    ch.sync()
                    A(v[s]["t1"], v[s]["t1"], ACT.Exp, scale=-0.5)
                    A(v[s]["t2"], v[s]["t2"], ACT.Exp, scale=-0.5)
                    act.wait_ge(dn["expo"], n + 1)
                    A(v[s]["eg"], B[2][:], ACT.Exp).then_inc(dn["scales"], 1)
                    A(v[s]["lt"], v[s]["lt"], ACT.Exp)
                    A(v[s]["ecol"], v[s]["ecol"], ACT.Exp).then_inc(dn["decay"], 1)
                for s in range(sets):
                    n, B = n0 + s, bank[4 * s:4 * s + 4]
                    act.wait_ge(dn["kk"], n + 1)
                    A(v[s]["vt"], B[2][:], ACT.Copy).then_inc(dn["vt"], 1)
                for s in range(sets):
                    n, B = n0 + s, bank[4 * s:4 * s + 4]
                    act.wait_ge(dn["x_t"], n + 1)
                    A(v[s]["x"], B[2][:], ACT.Copy).then_inc(dn["x0"], 1)
                if sets == 2:
                    for s in range(2):
                        act.wait_ge(dn["ident_minus"], n0 + s + 1)
                        dn_load(n0 + 2 + s, s, False)
                for lev in range(1, LEVELS):
                    at = n0 * (LEVELS - 1) + (lev - 1) * sets
                    for s in range(sets):
                        act.wait_ge(dn["p"], at + s + 1)
                        A(v[s]["t2"], bank[4 * s][:], ACT.Copy).then_inc(dn["p_sb"], 1)
                    for s in range(sets):
                        act.wait_ge(dn["u_t"], at + s + 1)
                        A(v[s]["u"], bank[4 * s + 2][:], ACT.Copy).then_inc(dn["u_sb"], 1)
                for s in range(sets):
                    n, B = n0 + s, bank[4 * s:4 * s + 4]
                    act.wait_ge(dn["vn"], n + 1)
                    A(v[s]["t2"], B[1][:], ACT.Copy).then_inc(dn["vn_sb"], 1)
                    act.wait_ge(dn["o"], n + 1)
                    for h in range(HEADS):
                        hs = slice(h * P, h * P + P)
                        last = A(v[s]["x"][:, hs], B[2][:, hs], ACT.Square, accum_out=v[s]["ss"][:, h:h + 1])
                    ch(last)
                    ch.sync()
                    ch(A(v[s]["ss"], v[s]["ss"], ACT.Ln, scale=1.0 / HD, bias=eps_col))
                    ch.sync()
                    A(v[s]["ss"], v[s]["ss"], ACT.Exp, scale=-0.5).then_inc(dn["o_scale"], 1)
                for s in range(sets):
                    n = n0 + s
                    act.wait_ge(dn["o_gated"], n + 1)
                    A(x_hi[:, 0:HEADS, bass.ds(n * P, width)], h4(v[s]["t1"])[:, :, 0:width], ACT.Copy
                      ).then_inc(dn["o_hi"], 1)
                    if sets == 2:
                        dn_load(n0 + 2 + s, s, True)

            with act.Fori(0, (BLOCKS - 1) // 2) as i:
                ch.enter(i, 0, 6)
                dn_act_blocks(2 * i, i, 2)
            ch.leave((BLOCKS - 1) // 2)
            dn_act_blocks(BLOCKS - 1, (BLOCKS - 1) // 2, 1, TAIL)
            act.wait_ge(dn["qkv_loaded1"], 48 * 5)
            act.wait_ge(dn["z_loaded1"], 16 * 5)

            sv = sb_views(carve)
            act.wait_ge(dn["out"], BLOCKS + 2)

            def load_head(hd):
                for m, x in ((SV, "v"), (SQ, "q"), (SK, "k")):
                    act.dma_start(sv[x], proj[m + hd][:, 0:T]).then_inc(sk["loaded"], 16)

            def sb_head(hd, more):
                w0 = hd * WT_GROUPS
                for g in range(3):
                    act.wait_ge(sk["w_t"], w0 + g + 1)
                    k = slice(0, P) if g < 2 else slice(0, TAIL)
                    w = 4 * P if g < 2 else P
                    A(sv["vt"][k, 4 * g * P:4 * g * P + w], bank[4 + g % 2][k, 0:w], ACT.Copy).then_inc(sk["wt_sb"], 1)
                for i in range(BLOCKS + 3):
                    if i == BLOCKS and more:
                        act.wait_ge(sk["z"], (hd + 1) * BLOCKS + 1)
                        load_head(hd + 1)
                    if i < BLOCKS:
                        nq, nk = min(P, T - i * P), min(T, (i + 1) * P)
                        e = sv["e"][i % 3]
                        act.wait_ge(sk["z"], hd * BLOCKS + i + 2)
                        for a in range(0, nk, 512):
                            m = min(512, nk - a)
                            last = A(e[0:nq, a:a + m], bank[(2 * (i % 2) + a // 512) % 4][0:nq, 0:m], ACT.Abs)
                        ch(last)
                        ch.sync()
                        ch(A(e[0:nq, 0:nk], e[0:nq, 0:nk], ACT.Exp, scale=-1.0))
                        ch.sync()
                        A(e[0:nq, 0:nk], e[0:nq, 0:nk], ACT.Ln, bias=1.0).then_inc(sk["soft"], 1)
                    if 0 < i <= BLOCKS:
                        nq, nk = min(P, T - (i - 1) * P), min(T, i * P)
                        e = sv["e"][(i - 1) % 3]
                        act.wait_ge(sk["logw"], hd * BLOCKS + i + 2)
                        A(e[0:nq, 0:nk], e[0:nq, 0:nk], ACT.Exp).then_inc(sk["w"], 1)
                    if i > 2:
                        sb_high(hd, i - 3)
                    if 1 < i < BLOCKS + 2:
                        sb_evac(hd, i - 2, w0)

            def sb_evac(hd, i, w0):
                nq = min(P, T - i * P)
                for gi, j0 in enumerate(range(0, i + 1, 4)):
                    nj = min(4, i + 1 - j0)
                    act.wait_ge(sk["w_t"], w0 + 3 + WT_BEFORE[i] + gi + 1)
                    if gi == 0:
                        act.wait_ge(sk["o"], hd * BLOCKS + i + 2)
                    src = bank[4 + (3 + WT_BEFORE[i] + gi) % 2]
                    k = slice(0, TAIL) if j0 == BLOCKS - 1 else slice(0, P)
                    A(sv["wt"][k, j0:j0 + nj, 0:nq],
                      src[k, 0:nj * P].rearrange("p (j q) -> p j q", j=nj)[:, :, 0:nq], ACT.Copy).then_inc(sk["wt_sb"], 1)

            def sb_high(hd, i):
                nq = min(P, T - i * P)
                act.wait_ge(sk["o"], hd * BLOCKS + i + 3)
                A(x_hi[:, HEADS + hd, i * P:i * P + nq], bank[6 + i % 2][:, 0:nq], ACT.Copy).then_inc(sk["o_hi"], 1)

            load_head(0)
            with act.Fori(0, HEADS - 1) as hd:
                ch.enter(hd, 0, 2 * BLOCKS)
                sb_head(hd, True)
            ch.leave(HEADS - 1)
            sb_head(HEADS - 1, False)

            act.wait_ge(sk["o_lo"], HEADS * BLOCKS + 2)
            with act.Fori(0, 2) as i:
                for s in range(4):
                    for c, (a, n) in enumerate(CUTS):
                        act.wait_ge(group_done, GROUPS_BEFORE["w_out"] + 12 * i + 3 * s + c + 1)
                        last = A(acc[:, 4 * i + s, a:a + n], bank[(3 * s + c) % 6][:, 0:n], ACT.Copy)
                        last.then_inc(group_free, 1)
            residual_block(1, xT, resid[0])

            def ffn(layer):
                base = layer * PAIRS
                gate, f = ffn_views(carve)
                act.wait_ge(nm_stored[0], 16 * (2 + 4 * layer))
                act.wait_ge(nm_stored[1], 16 * (1 + 2 * layer))
                with act.Fori(0, PAIRS) as i:
                    for st in range(6):
                        a, n = CUTS[st // 2]
                        step = (base + i) * 6 + st
                        act.wait_ge(gu_done, step + 1)
                        act.wait_ge(act_f32, step + 1)
                        A(gate[st % 2][:, 0:n], bank[2 * (st % 2)][:, 0:n], ACT.Silu).then_inc(silu_done, 1)
                        act.wait_ge(act_f32, step + 3)
                        act.wait_ge(down_done, (base + i) * 24 + 1)
                        A(act_hi[:, st % 2, a:a + n], f[st % 2][:, 0:n], ACT.Copy).then_inc(act_high, 1)
                act.wait_ge(act_ready, 6 * (base + PAIRS))

            act.sem_inc(down_done, 1)
            ffn(0)
            residual_block(2, resid[0], resid[1])

            z = s5_views(carve)
            act.wait_ge(x_ready, 9)
            act.wait_ge(nm_stored[0], 16 * 4)
            act.wait_ge(nm_stored[1], 16 * 2)
            act.dma_start(z["par"], s5_in).then_inc(s5["params"], 16)
            act.wait_ge(s5["params"], 16)
            A(z["dt"], z["par"][:, S_LOG:S_LOG + 32], ACT.Exp).then_inc(s5["act"], 1)
            act.wait_ge(s5["angles"], 1)
            A(z["mag"], z["lr"], ACT.Exp)
            A(z["mag8"], z["lr"], ACT.Exp, scale=float(CH))
            A(z["sin"], z["ang"], ACT.Sin)
            A(z["half"], z["ang"], ACT.Sin, scale=0.5).then_inc(s5["act"], 1)
            with act.Fori(0, 2) as i:
                for c, (a, n) in enumerate(CUTS):
                    for j in range(4):
                        g = GROUPS_BEFORE["ssm_in"] + 12 * i + 4 * c + j
                        if c == 0:
                            act.wait_ge(u_stored[j], 16 * (i + 1))
                        act.wait_ge(group_done, g + 1)
                        A(z["ut"][j].rearrange("p (s j) -> p j s", s=CH)[:, a // CH:(a + n) // CH, :],
                          bank[(4 * c + j) % 6][:, 0:n].rearrange("p (j s) -> p j s", s=CH), ACT.Copy
                          ).then_inc(group_free, 1)
                        if c == 2:
                            act.wait_ge(group_free, 6 + g + 1)
                            act.dma_start(s5_u[4 * i + j].rearrange("s c j -> c s j"),
                                          z["ut"][j].rearrange("p (s j) -> p s j", s=CH)).then_inc(u_stored[j], 16)

            def s5_tile(m, tail):
                act.wait_ge(s5["win_t"], m + 1)
                for part in range(2):
                    last = A(z["win"][part].rearrange("p q s -> p (q s)"), bank[part][:], ACT.Copy)
                last.then_inc(s5["win_sb"], 1)
                act.wait_ge(s5["t_done"], m + 1)
                for t2 in range(2):
                    for t in range(4):
                        last = A(z["t"].rearrange("p g (t c) -> p g t c", t=CH)[:, :, 4 * t2 + t, :],
                                 bank[4 + t2][:, t * P:t * P + P].rearrange("p (g c) -> p g c", g=GPT), ACT.Copy)
                last.then_inc(s5["t_sb"], 1)
                act.wait_ge(s5["v"], m + 1)
                for part in range(2):
                    for qh in range(2):
                        last = A(z["v"][part][:, 2 * qh:2 * qh + 2, :],
                                 bank[2 * part + qh][:, 0:2 * NJ].rearrange("p (q j) -> p q j", q=2), ACT.Copy)
                last.then_inc(s5["v_sb"], 1)
                if tail:
                    s5_tail(m - 1)
                act.wait_ge(s5["y"], m + 2)
                act.wait_ge(s5["y_free"], m + 1)
                for qh in range(2):
                    for b in range(2):
                        last = A(z["y"].rearrange("p (q b) j -> p q b j", b=2)[:, 2 * qh:2 * qh + 2, b, :],
                                 bank[4 + 2 * qh + b][:, 0:2 * NJ].rearrange("p (q j) -> p q j", q=2), ACT.Copy)
                last.then_inc(s5["y_sb"], 1)

            def s5_tail(m):
                act.wait_ge(s5["y_loaded"], (m + 1) * 16)
                A(z["yh"], z["yh"], ACT.Gelu_apprx_tanh).then_inc(s5["gelu"], 1)
                act.wait_ge(s5["gelu"], m + 1)
                A(x_hi[:, m, :].rearrange("p (j s) -> p s j", s=CH), z["yh"].rearrange("p (s j) -> p s j", s=CH),
                  ACT.Copy).then_inc(s5["hi"], 1)

            act.sem_inc(s5["y"], 1)
            act.sem_inc(s5["y_sb"], 1)
            for i in range(4):
                act.wait_ge(u_stored[i], 16 * 3)
            s5_tile(0, False)
            with act.Fori(1, KT) as m:
                s5_tile(m, True)
            s5_tail(KT - 1)

            gate, _f = ffn_views(carve)
            act.wait_ge(s5["lo"], KT + 1)
            with act.Fori(0, 4) as i:
                for j in range(2):
                    for c, (a, n) in enumerate(CUTS):
                        at = 6 * i + 3 * j + c
                        act.wait_ge(group_done, GROUPS_BEFORE["glu"] + 2 * at + 2)
                        act.wait_ge(glu_mul, at + 2)
                        A(gate[(3 * j + c) % 2][:, 0:n], bank[2 * c + 1][:, 0:n], ACT.Sigmoid).then_inc(glu_gate, 1)
            act.wait_ge(glu_mul, 24 + 3)
            residual_block(3, resid[1], resid[2])
            ffn(1)
            residual_block(4, resid[2], outT)
            act.wait_ge(nm_stored[0], 16 * 8)
            act.wait_ge(nm_stored[1], 16 * 4)

        @block.vector
        def _(dve):
            V = nc.vector
            ch = Chain(dve, dve_chain_sem)
            mul, sub, add = ALU.mult, ALU.subtract, ALU.add

            def residual_block(r, pre_w, post_w):
                for c, m in norm_steps(r):
                    a, n = CUTS[c]
                    p, e = 3 * r + c, norm_event(r, c, m)
                    h, nb, rr = nv["h"][c % 2][:, :, 0:n], nv["nb"][:, :, 0:n], nv["rs"][e % 2][:, 0:n]
                    dve.wait_ge(nm_root, e + 1)
                    ch(V.reciprocal(rr, rr))
                    ch.sync()
                    if m == 0:
                        for k in range(KT):
                            last = V.scalar_tensor_tensor(out=acc[:, k, a:a + n], in0=acc[:, k, a:a + n],
                                                          scalar=small[:, post_w + k:post_w + k + 1],
                                                          in1=rr, op0=mul, op1=mul)
                        ch(last)
                        ch.sync()
                        dve.wait_ge(nm_loaded[c % 2], 16 * (r + 1 if c == 1 else 2 * r + c // 2 + 1))
                        V.tensor_tensor(h, h, acc[:, :, a:a + n], add).then_inc(nm_resid, 1)
                    else:
                        if p > 0:
                            dve.wait_ge(x_ready, p)
                        for k in range(KT):
                            last = V.scalar_tensor_tensor(out=nb[:, k, :], in0=h[:, k, :],
                                                          scalar=small[:, pre_w + k:pre_w + k + 1],
                                                          in1=rr, op0=mul, op1=mul)
                        last.then_inc(nm_normed, 1)
                        dve.wait_ge(nm_high, p + 1)
                        V.tensor_tensor(x_lo[:, :, a:a + n], nb, x_hi[:, :, a:a + n].bitcast(F32), sub).then_inc(x_ready, 1)

            V.memset(sb_eps[:, 0:1], EPS).then_inc(eps_ready, 1)
            V.memset(sb_eps[:, 1:2], EPS * HD).then_inc(eps_ready, 1)
            V.memset(carve(18300, T_PAD - T), 0.0).then_inc(eps_ready, 1)
            for s_, k_ in ((act_f32, 2), (down_free, 4), (conv_done, 2), (dn["out"], 2), (sk["logw"], 2), (sk["o_lo"], 2),
                           (glu_mul, 3), (proj_out, 2)):
                for _i in range(k_):
                    dve.sem_inc(s_, 1)
            dve.wait_ge(params_loaded, 32)
            residual_block(0, MIX_PRE, None)

            rows = carve(0, T_ROWS)
            ga, gb, keep = carve(T_ROWS, T_ROWS), carve(2 * T_ROWS, T_ROWS), carve(3 * T_ROWS, T_ROWS)
            cb, ct, po = conv_views(carve)
            ch(V.memset(rows, 0.0))
            ch(V.memset(ga, 0.0))
            ch(V.memset(keep, 1.0))
            ch.sync()
            ch(V.memset(keep.rearrange("p (b t) -> p b t", t=P)[:, :, 0:1], 0.0))
            for i in range(2):
                ch(V.memset(cb[i][:, 0:3], 0.0))
            ch.sync()
            V.memset(gb, 0.0).then_inc(gate_dve, 1)
            dve.wait_ge(gate_act, 1)
            ch(V.tensor_scalar(rows[32:36, 0:T], rows[32:36, 0:T], 1.0, None, add))
            ch.sync()
            V.reciprocal(rows[32:36, 0:T], rows[32:36, 0:T]).then_inc(gate_dve, 1)
            ch(V.scalar_tensor_tensor(out=ga[0:4, 0:T], in0=ga[0:4, 0:T], scalar=0.0, in1=gb[0:4, 0:T], op0=ALU.max, op1=add))
            ch.sync()
            ch(V.tensor_scalar(ga[0:4, 0:T], ga[0:4, 0:T], gate_col[0:4, :], -1.0, mul, mul))
            ch.sync()
            V.tensor_tensor_scan(rows[0:4, :], keep[0:4, :], ga[0:4, :], 0.0, mul, add).then_inc(gate_dve, 1)

            with dve.Fori(0, 3) as i:
                ch.enter(i, 0, 12)
                for s in range(4):
                    u, par = 4 * i + s, s % 2
                    dve.wait_ge(group_free, 12 + 3 * u + 3)
                    dve.wait_ge(proj_out, u + 1)
                    ch(V.tensor_scalar(ct[par], cb[par][:, 3:3 + T], small[:, bass.ds(W_CONV + 4 * u + 3, 1)], None, mul))
                    for j in (2, 1, 0):
                        ch.sync()
                        ins = V.scalar_tensor_tensor(out=ct[par], in0=cb[par][:, j:j + T],
                                                     scalar=small[:, bass.ds(W_CONV + 4 * u + j, 1)], in1=ct[par],
                                                     op0=mul, op1=add)
                        if j:
                            ch(ins)
                    ins.then_inc(conv_done, 1)
            ch.leave(3)

            v = dn_views(carve)
            dve.wait_ge(cols_ready, 1)
            V.memset(v["state"], 0.0).then_inc(dn["state"], 1)

            def per_head(f):
                for h in range(HEADS):
                    last = f(h, slice(h * P, h * P + P))
                return last

            def dn_blocks(n0, sets, width=P):
                for s in range(sets):
                    n, B, w = n0 + s, bank[4 * s:4 * s + 4], v[s]
                    dve.wait_ge(dn["bcast"], n + 1)
                    g_col = lambda h: v["cols"][:, n, h:h + 1]
                    per_head(lambda h, hs: V.tensor_scalar(w["lt"][:, hs], B[2][:, hs], g_col(h), 0.0, sub, ALU.min))
                    V.tensor_tensor(w["ecol"], h4(B[2][:])[:, :, P - 1], v["cols"][:, n, 0:HEADS], sub
                                    ).then_inc(dn["expo"], 1)
                    dve.wait_ge(dn["scales"], n + 1)
                    ch(V.tensor_tensor(w["k"], w["k"], w["t1"], mul))
                    ch(V.tensor_tensor(w["v"], w["v"], B[3][:], mul))
                    ch(V.tensor_tensor(w["q"], w["q"], w["t2"], mul))
                    V.tensor_copy(w["gl"], h4(w["eg"])[:, :, P - 1])
                    ch.sync()
                    V.tensor_tensor(w["kb"], w["k"], B[3][:], mul).then_inc(dn["kq"], 1)
                    V.tensor_tensor(w["qd"], w["q"], w["eg"], mul).then_inc(dn["qd"], 1)
                for s in range(sets):
                    n, B, w = n0 + s, bank[4 * s:4 * s + 4], v[s]
                    dve.wait_ge(dn["decay"], n + 1)
                    dve.wait_ge(dn["kk"], n + 1)
                    ch(V.tensor_tensor(w["kd"], B[0][:], w["lt"], mul))
                    ch.sync()
                    ch(V.tensor_tensor(h4(w["t1"]), h4(w["kd"]), over_heads(level(0)), mul))
                    ch.sync()
                    V.tensor_tensor(h4(w["u"]), over_heads(ident), h4(w["t1"]), sub).then_inc(dn["ident_minus"], 1)
                    ch(V.tensor_tensor(w["qk"], B[1][:], w["lt"], mul))

                def mask(s, lev):
                    V.tensor_tensor(h4(v[s]["t1"]), h4(v[s]["kd"]), over_heads(level(lev)), mul).then_inc(dn["masked"], 1)

                def meanwhile(lev):
                    for s in range(sets):
                        w, B = v[s], bank[4 * s:4 * s + 4]
                        if lev == 1:
                            V.tensor_tensor(w["kb"], w["kb"], w["eg"], mul)
                        if lev == 2:
                            V.tensor_tensor(h4(w["qk"]), h4(w["qk"]), over_heads(incl), mul)
                        if lev == LEVELS - 1:
                            dve.wait_ge(dn["masked"], (n0 + sets) * (LEVELS - 1))
                            per_head(lambda h, hs: V.tensor_scalar(w["kd"][:, hs], B[3][:, hs], w["ecol"][:, h:h + 1],
                                                                   None, mul))

                for s in range(sets):
                    dve.wait_ge(dn["ident_minus"], n0 + s + 1)
                    mask(s, 1)
                for lev in range(1, LEVELS):
                    at = n0 * (LEVELS - 1) + (lev - 1) * sets
                    if lev + 1 < LEVELS:
                        for s in range(sets):
                            dve.wait_ge(dn["p"], at + s + 1)
                            mask(s, lev + 1)
                    for s in range(sets):
                        dve.wait_ge(dn["up"], at + s + 1)
                        V.tensor_tensor(v[s]["x"], v[s]["x"], bank[4 * s + 1][:], sub).then_inc(dn["x_new"], 1)
                    meanwhile(lev)
                for s in range(sets):
                    n, B, w = n0 + s, bank[4 * s:4 * s + 4], v[s]
                    dve.wait_ge(dn["ks"], n + 1)
                    V.tensor_tensor(w["t1"], w["vt"], B[0][:], sub).then_inc(dn["rhs"], 1)
                    dve.wait_ge(dn["o"], n + 1)
                    per_head(lambda h, hs: V.scalar_tensor_tensor(
                        out=v["state"][:, hs], in0=v["state"][:, hs], scalar=w["gl"][:, h:h + 1], in1=B[3][:, hs],
                        op0=mul, op1=add)).then_inc(dn["state"], 1)
                    dve.wait_ge(dn["o_scale"], n + 1)
                    per_head(lambda h, hs: V.tensor_scalar(w["x"][:, hs], B[2][:, hs], w["ss"][:, h:h + 1], None, mul)
                             ).then_inc(dn["o_norm"], 1)
                for s in range(sets):
                    n, B, w = n0 + s, bank[4 * s:4 * s + 4], v[s]
                    dve.wait_ge(dn["o_t"], n + 1)
                    dve.wait_ge(dn[f"z_loaded{s}"], 16 * (z_turn[0] + 1))
                    V.scalar_tensor_tensor(out=w["t1"], in0=B[0][:], scalar=small[:, W_ONORM:W_ONORM + 1], in1=w["z"],
                                           op0=mul, op1=mul).then_inc(dn["o_gated"], 1)
                    dve.wait_ge(dn["o_hi"], n + 1)
                    at = bass.ds(n * P, width)
                    V.tensor_tensor(x_lo[:, 0:HEADS, at], h4(w["t1"])[:, :, 0:width],
                                    x_hi[:, 0:HEADS, at].bitcast(F32), sub).then_inc(dn["out"], 1)

            z_turn = [0]
            with dve.Fori(0, (BLOCKS - 1) // 2) as i:
                z_turn[0] = i
                ch.enter(i, 0, 12)
                dn_blocks(2 * i, 2)
            ch.leave((BLOCKS - 1) // 2)
            z_turn[0] = (BLOCKS - 1) // 2
            dn_blocks(BLOCKS - 1, 1, TAIL)

            sv = sb_views(carve)

            def sb_mask(hd, i):
                nq, d0, nk = min(P, T - i * P), i * P, min(T, (i + 1) * P)
                e = sv["e"][i % 3]
                dve.wait_ge(sk["w"], hd * BLOCKS + i + 1)
                V.tensor_tensor(e[0:nq, d0:nk], e[0:nq, d0:nk], strict[0:nq, 0:nk - d0], mul).then_inc(sk["wm"], 1)

            def sb_low(hd, i):
                nq = min(P, T - i * P)
                dve.wait_ge(sk["o_hi"], hd * BLOCKS + i + 1)
                o = slice(i * P, i * P + nq)
                V.tensor_tensor(x_lo[:, HEADS + hd, o], bank[6 + i % 2][:, 0:nq], x_hi[:, HEADS + hd, o].bitcast(F32), sub
                                ).then_inc(sk["o_lo"], 1)

            with dve.Fori(0, HEADS) as hd:
                ch.enter(hd, 0, 4 * BLOCKS)
                for i in range(BLOCKS):
                    nq, nk = min(P, T - i * P), min(T, (i + 1) * P)
                    e, r, d0 = sv["e"][i % 3], sv["r"][i % 2], i * P
                    src = lambda a: bank[(2 * (i % 2) + a // 512) % 4]
                    pieces = [(a, min(512, nk - a)) for a in range(0, nk, 512)]
                    dve.wait_ge(sk["soft"], hd * BLOCKS + i + 1)
                    for a, m in pieces:
                        last = V.scalar_tensor_tensor(out=r[0:nq, a:a + m], in0=src(a)[0:nq, 0:m], scalar=0.0,
                                                      in1=e[0:nq, a:a + m], op0=ALU.max, op1=add)
                    ch(last)
                    ch.sync()
                    ch(V.tensor_tensor(r[0:nq, d0:nk], r[0:nq, d0:nk], strict[0:nq, 0:nk - d0], mul))
                    ch.sync()
                    rv = r[0:nq, nk - 1::-1] if nk == T else r[0:nq, 0:nk][:, ::-1]
                    ch(V.tensor_tensor_scan(rv, rv, rv, 0.0, add, ALU.max))
                    ch.sync()
                    for a, m in pieces:
                        last = V.tensor_tensor(e[0:nq, a:a + m], src(a)[0:nq, 0:m], r[0:nq, a:a + m], sub)
                    ch(last)
                    ch.sync()
                    V.tensor_scalar(e[0:nq, d0:nk], e[0:nq, d0:nk], 0.0, None, ALU.min).then_inc(sk["logw"], 1)
                    if i > 0:
                        sb_mask(hd, i - 1)
                    if i > 2:
                        sb_low(hd, i - 3)
                sb_mask(hd, BLOCKS - 1)
                sb_low(hd, BLOCKS - 3)
                sb_low(hd, BLOCKS - 2)
                sb_low(hd, BLOCKS - 1)
            ch.leave(HEADS)

            residual_block(1, FFN_PRE, MIX_POST)

            def ffn(layer):
                base = layer * PAIRS
                gate, f = ffn_views(carve)

                def pair(i, first):
                    for st in range(6):
                        a, n = CUTS[st // 2]
                        step = (base + i) * 6 + st
                        dve.wait_ge(silu_done, step + 1)
                        V.tensor_tensor(f[st % 2][:, 0:n], gate[st % 2][:, 0:n], bank[2 * (st % 2) + 1][:, 0:n], mul
                                        ).then_inc(act_f32, 1)
                        dve.wait_ge(act_high, step + 1)
                        V.tensor_tensor(act_lo[:, st % 2, a:a + n], f[st % 2][:, 0:n],
                                        act_hi[:, st % 2, a:a + n].bitcast(F32), sub).then_inc(act_ready, 1)
                    for c, (a, n) in enumerate(CUTS):
                        for m in range(KT):
                            dve.wait_ge(down_done, (base + i) * 24 + 8 * c + m + 2)
                            o, src = acc[:, m, a:a + n], bank[4 + m % 4][:, 0:n]
                            last = V.tensor_copy(o, src) if first else V.tensor_tensor(o, o, src, add)
                            last.then_inc(down_free, 1)

                pair(0, True)
                with dve.Fori(1, PAIRS) as i:
                    pair(i, False)

            ffn(0)
            residual_block(2, MIX_PRE + 8, FFN_POST)

            z = s5_views(carve)
            par = z["par"]
            lre, lim = par[:, S_LRE:S_LRE + 32], par[:, S_LIM:S_LIM + 32]
            tt = lambda o, a, b, op: ch(V.tensor_tensor(o, a, b, op))

            def cmul(ore, oim, are, aim, bre, bim, t0, t1, conj=False):
                ch.sync()
                tt(t0, aim, bim, mul)
                tt(t1, aim, bre, mul)
                tt(ore, are, bre, mul)
                tt(oim, are, bim, mul)
                ch.sync()
                tt(ore, ore, t0, add if conj else sub)
                tt(oim, oim, t1, sub if conj else add)
                ch.sync()

            dve.wait_ge(s5["act"], 1)
            tt(z["lr"], lre, z["dt"], mul)
            tt(z["ta"], lim, z["dt"], mul)
            ch.sync()
            ch(V.tensor_scalar(z["turns"], z["ta"], float(1 / (2 * np.pi)), None, mul))
            ch.sync()
            ch(V.tensor_copy(z["tb"], z["turns"]))
            ch.sync()
            for part in (TWO_PI_A, TWO_PI_B, TWO_PI_C):
                ch(V.scalar_tensor_tensor(out=z["ta"], in0=z["tb"], scalar=-part, in1=z["ta"], op0=mul, op1=add))
                ch.sync()
            V.tensor_scalar(z["ang"], z["ta"], 3.1415925, -3.1415925, ALU.min, ALU.max).then_inc(s5["angles"], 1)
            dve.wait_ge(s5["act"], 2)
            tt(z["ta"], z["half"], z["half"], mul)
            ch.sync()
            ch(V.tensor_scalar(z["cos"], z["ta"], -2.0, 1.0, mul, add))
            ch.sync()
            p_re, p_im = z["pw"]
            ch(V.memset(p_re[:, 0, :], 1.0))
            ch(V.memset(p_im[:, 0, :], 0.0))
            tt(p_re[:, 1, :], z["mag"], z["cos"], mul)
            tt(p_im[:, 1, :], z["mag"], z["sin"], mul)
            tt(z["ta"], lre, lre, mul)
            tt(z["tb"], lim, lim, mul)
            ch.sync()
            tt(z["den"], z["ta"], z["tb"], add)
            ch(V.tensor_scalar(z["are"], p_re[:, 1, :], -1.0, None, add))
            ch.sync()
            ch(V.reciprocal(z["den"], z["den"]))
            cmul(z["fre"], z["fim"], lre, lim, z["are"], p_im[:, 1, :], z["ta"], z["tb"], conj=True)
            tt(z["fre"], z["fre"], z["den"], mul)
            tt(z["fim"], z["fim"], z["den"], mul)
            ch.sync()
            wide = lambda x: x.rearrange("p (q c) -> p q c", c=1).to_broadcast([P, S_PAIRS, G_CH])
            b3 = lambda at: par[:, at:at + 512].rearrange("p (q c) -> p q c", c=G_CH)
            bre, bim, cre, cim = (b3(x) for x in (S_BRE, S_BIM, S_CRE, S_CIM))
            ch.sync()
            fre, fim = wide(z["fre"]), wide(z["fim"])
            t0, t1 = (x.rearrange("p (q c) -> p q c", c=G_CH) for x in z["tmp"])
            t2 = z["m"][0].rearrange("p q (a c) -> p (q a) c", c=G_CH)
            tt(t0, fim, bim, mul)
            tt(t1, fim, bre, mul)
            tt(t2, fre, bim, mul)
            ch.sync()
            tt(bre, fre, bre, mul)
            tt(bim, t2, t1, add)
            ch.sync()
            tt(bre, bre, t0, sub)
            sm = lambda x, n, w: x.rearrange("p (n w) -> p n w", w=w)[:, 0:n, :]
            for have in (1, 2, 4):
                o = slice(have + 1, 2 * have + 1)
                by = lambda p: p[:, have:have + 1, :].to_broadcast([P, have, S_PAIRS])
                cmul(p_re[:, o, :], p_im[:, o, :], by(p_re), by(p_im), p_re[:, 1:have + 1, :], p_im[:, 1:have + 1, :],
                     sm(z["tmp"][0], have, S_PAIRS), sm(z["tmp"][1], have, S_PAIRS))
            for part in range(2):
                for s in range(CH):
                    ch(V.tensor_copy(z["pr"][part][:, s, :], z["pw"][part][:, CH - 1 - s, :]))

            c_re, c_im = z["cos"], z["sin"]
            for _i in range(3):
                cmul(z["ta"], z["tb"], c_re, c_im, c_re, c_im, z["fre"], z["fim"])
                ch(V.tensor_copy(c_re, z["ta"]))
                ch(V.tensor_copy(c_im, z["tb"]))
                ch.sync()
            for tab, size in ((z["ph_b"], 16), (z["ph_a"], 9)):
                re, im = tab
                ch(V.memset(re[:, :, 0:1], 1.0))
                ch(V.memset(im[:, :, 0:1], 0.0))
                ch(V.tensor_copy(re[:, :, 1:2], c_re.rearrange("p (q o) -> p q o", o=1)))
                ch(V.tensor_copy(im[:, :, 1:2], c_im.rearrange("p (q o) -> p q o", o=1)))
                ch.sync()
                have = 1
                while have < size - 1:
                    more = min(have, size - 1 - have)
                    by = lambda p: p[:, :, have:have + 1].to_broadcast([P, S_PAIRS, more])
                    cmul(re[:, :, have + 1:have + 1 + more], im[:, :, have + 1:have + 1 + more], by(re), by(im),
                         re[:, :, 1:1 + more], im[:, :, 1:1 + more],
                         sm(z["tmp"][0], S_PAIRS, G_CH)[:, :, 0:more], sm(z["tmp"][1], S_PAIRS, G_CH)[:, :, 0:more])
                    have += more
                if size == 16:
                    cmul(z["ta"], z["tb"], re[:, :, 15], im[:, :, 15], c_re, c_im, z["fre"], z["fim"])
                    c_re, c_im = z["ta"], z["tb"]
            for part in range(2):
                ch(V.memset(z["x"][part][:, :, 0:1], 0.0))
            ch.sync()

            def s5_tile(m, tail):
                qs = bass.ts(m, QP)
                w4 = [P, QP, CH, G_CH]
                a_in = lambda p: p[:, 0:CH, qs].rearrange("p s (q c) -> p q s c", c=1).to_broadcast(w4)
                a_out = lambda p: p[:, 1:1 + CH, qs].rearrange("p s (q c) -> p q s c", c=1).to_broadcast(w4)
                bc = lambda x: x[:, qs, :].rearrange("p q (s c) -> p q s c", s=1).to_broadcast(w4)
                v4 = lambda x: x.rearrange("p q (s c) -> p q s c", s=CH)
                t0, t1 = z["t128"]
                cmul(v4(z["m"][0]), v4(z["m"][1]), a_in(z["pr"][0]), a_in(z["pr"][1]), bc(bre), bc(bim), v4(t0), v4(t1))
                ch(V.tensor_copy(z["cc"][0], cre[:, qs, :]))
                ch.sync()
                V.tensor_scalar(z["cc"][1], cim[:, qs, :], -1.0, None, mul).then_inc(s5["win"], 1)
                d3 = par[:, bass.ds(S_D + m * GPT, GPT)].rearrange("p (g c) -> p g c", c=1).to_broadcast([P, GPT, G_CH])
                lag0 = ident[:, P - G_CH:P].rearrange("p (g c) -> p g c", g=1).to_broadcast([P, GPT, G_CH])
                tt(z["dd"], d3, lag0, mul)
                dve.wait_ge(s5["y"], m + 1)
                cmul(v4(z["wout"][0]), v4(z["wout"][1]), a_out(p_re), a_out(p_im), bc(cre), bc(cim), v4(t0), v4(t1))
                ch(V.tensor_scalar(z["wout"][1], z["wout"][1], -1.0, None, mul))
                dve.wait_ge(s5["k"], m + 1)
                of = lambda x, b: x.rearrange("p (q b) c -> p q b c", b=2)[:, :, b, :]
                for b in range(2):
                    last = V.tensor_tensor(of(z["k"].rearrange("p (g c) -> p g c", g=GPT), b),
                                           bank[2 + b][:, 0:QP * G_CH].rearrange("p (q c) -> p q c", q=QP),
                                           of(z["dd"], b), add)
                last.then_inc(s5["k_sb"], 1)
                w4 = [P, QP, 9, 16]
                pa = lambda p: p[:, qs, :].rearrange("p q (a o) -> p q a o", o=1).to_broadcast(w4)
                pb = lambda p: p[:, qs, :].rearrange("p q (o b) -> p q o b", o=1).to_broadcast(w4)
                o4 = lambda x: x.rearrange("p q (a b) -> p q a b", b=16)
                t0, t1 = z["t144"]
                cmul(o4(z["ph"][0]), o4(z["ph"][1]), pa(z["ph_a"][0]), pa(z["ph_a"][1]), pb(z["ph_b"][0]),
                     pb(z["ph_b"][1]), o4(t0), o4(t1))
                ch(V.tensor_copy(z["m8"], z["mag8"][:, qs].rearrange("p (q o) -> p q o", o=1).to_broadcast([P, QP, NJ])))
                ch.sync()
                ch(V.memset(z["m8"][:, :, 0:1], 0.0))
                dve.wait_ge(s5["v_sb"], m + 1)
                f_re, f_im = (x[:, :, 0:NJ] for x in z["ph"])
                r = z["rot"]
                cmul(r[0], r[1], f_re, f_im, z["v"][0], z["v"][1], r[2], r[3], conj=True)
                flat = lambda x: x.rearrange("p q j -> p (q j)")
                for part in range(2):
                    ch(V.tensor_tensor_scan(flat(z["v"][part]), flat(z["m8"]), flat(r[part]), 0.0, mul, add))
                ch.sync()
                x_re, x_im = (x[:, :, 1:NJ + 1] for x in z["x"])
                tt(r[2], f_im, z["v"][1], mul)
                tt(r[3], f_im, z["v"][0], mul)
                tt(x_re, f_re, z["v"][0], mul)
                tt(x_im, f_re, z["v"][1], mul)
                ch.sync()
                ch(V.tensor_tensor(x_re, x_re, r[2], sub))
                ch(V.tensor_tensor(x_im, x_im, r[3], add))
                ch.sync()
                dve.sem_inc(s5["x"], 1)
                if tail:
                    s5_low(m - 1)

            def s5_low(m):
                dve.wait_ge(s5["hi"], m + 1)
                dst = lambda x: x[:, m, :].rearrange("p (j s) -> p s j", s=CH)
                V.tensor_tensor(dst(x_lo), z["yh"].rearrange("p (s j) -> p s j", s=CH), dst(x_hi).bitcast(F32), sub
                                ).then_inc(s5["lo"], 1)

            dve.sem_inc(s5["lo"], 1)
            for i in range(4):
                dve.wait_ge(u_stored[i], 16 * 3)
            s5_tile(0, False)
            with dve.Fori(1, KT) as m:
                ch.enter(m, 1, S5_MARKS)
                s5_tile(m, True)
            ch.leave(KT - 1)
            s5_low(KT - 1)

            gate, _f = ffn_views(carve)
            with dve.Fori(0, 4) as i:
                for j in range(2):
                    for c, (a, n) in enumerate(CUTS):
                        dve.wait_ge(glu_gate, 6 * i + 3 * j + c + 1)
                        last = V.tensor_tensor(acc[:, 2 * i + j, a:a + n], bank[2 * c][:, 0:n],
                                               gate[(3 * j + c) % 2][:, 0:n], mul)
                        last.then_inc(glu_mul, 1)
            residual_block(3, FFN_PRE + 8, MIX_POST + 8)
            ffn(1)
            residual_block(4, None, FFN_POST + 8)


def kernel(**inputs):
    import concourse.bacc as bacc
    from concourse.bass_utils import run_bass_kernel_spmd

    f = {k: np.ascontiguousarray(v) for k, v in inputs.items()}
    assert all(v.dtype == np.float32 for v in f.values())

    def feature_major(x):
        return x.reshape(x.shape[0], -1, P).transpose(2, 1, 0)

    def slabs(w):
        return w.reshape(KT, P, -1, P).transpose(2, 1, 0, 3).reshape(-1, P, KT * P)

    def ffn_slabs(layer):
        gate, up = slabs(f["ffn_w_gate"][layer]), slabs(f["ffn_w_up"][layer])
        down = f["ffn_w_down"][layer].reshape(PAIRS, 2, P, 2, 512).transpose(0, 3, 2, 1, 4).reshape(PAIRS, 2, P, 1024)
        out = []
        for p in range(PAIRS):
            out += [gate[2 * p], up[2 * p], gate[2 * p + 1], up[2 * p + 1], down[p, 0], down[p, 1]]
        return np.stack(out)

    w_in = f["hyb_w_in"][0]
    da = HEADS * HD
    gates = np.zeros((D, P), np.float32)
    gates[:, 0:4] = w_in[:, 4 * da + 4:4 * da + 8]
    gates[:, 32:36] = w_in[:, 4 * da:4 * da + 4]
    glu = slabs(f["ssm_w_glu"][0])
    stream = np.concatenate([
        slabs(gates), slabs(w_in[:, :4 * da]), slabs(w_in[:, 4 * da + 8:]), slabs(f["hyb_w_out"][0]), ffn_slabs(0),
        slabs(f["ssm_w_in"][0]), np.stack([glu[:KT], glu[KT:]], axis=1).reshape(2 * KT, P, 1024), ffn_slabs(1)])
    assert stream.shape == (N_SLABS, P, 1024)

    small = np.zeros((P, N_SMALL), np.float32)
    for at, name in ((MIX_PRE, "norm_mix_pre"), (MIX_POST, "norm_mix_post"), (FFN_PRE, "norm_ffn_pre"),
                     (FFN_POST, "norm_ffn_post")):
        small[:, at:at + 16] = f[name].reshape(2 * KT, P).T
    small[:, W_CONV:W_CONV + 48] = f["hyb_conv_w"][0].reshape(4, 12, P).transpose(2, 1, 0).reshape(P, 48)
    small[:, W_ONORM] = f["dn_out_norm"][0]
    small[0:4, A_LOG] = f["dn_a_log"][0]
    small[0:4, DT_BIAS] = f["dn_dt_bias"][0]

    const = np.zeros((P, N_CONST), np.float32)
    i, j = np.meshgrid(np.arange(P), np.arange(P))
    const[:, C_ID:C_ID + P] = const[:, C_SHIFT:C_SHIFT + P] = i == j
    const[:, C_ONES:C_ONES + P] = 1
    const[:, C_INCL:C_INCL + P] = i >= j
    const[:, C_STRICT:C_STRICT + P] = i < j
    for lev in range(LEVELS):
        b = 1 << lev
        const[:, C_LEVEL + P * lev:C_LEVEL + P * lev + P] = (i // (2 * b) == j // (2 * b)) & (i // b % 2 == 1) & (j // b % 2 == 0)
    for h in range(HEADS):
        const[h, C_SEL + h * P:C_SEL + h * P + P] = 1
        const[32 + h, C_SEL + (4 + h) * P:C_SEL + (5 + h) * P] = 1

    def pairs(x):
        return x.reshape((S_PAIRS, 2 * STATE) + x.shape[2:]).swapaxes(0, 1)

    d_rows = np.zeros((P, N_GROUPS), np.float32)
    d_rows[P - G_CH:] = f["ssm_d"][0].reshape(N_GROUPS, G_CH).T
    s5 = np.concatenate([
        pairs(f["ssm_lambda_re"][0]), pairs(f["ssm_lambda_im"][0]),
        pairs(np.repeat(f["ssm_log_step"][0][:, None], STATE, axis=1)),
        pairs(f["ssm_b_re"][0]).reshape(P, -1), pairs(f["ssm_b_im"][0]).reshape(P, -1),
        pairs(f["ssm_c_re"][0].swapaxes(1, 2)).reshape(P, -1), pairs(f["ssm_c_im"][0].swapaxes(1, 2)).reshape(P, -1),
        d_rows],
        axis=1)
    assert s5.shape == (P, N_S5)

    arrays = {
        "xT": feature_major(np.concatenate([f["meta_tokens"], f["x"][0]])), "wstream": stream, "small_in": small,
        "const_in": const, "s5_in": s5}
    arrays = {k: np.ascontiguousarray(a) for k, a in arrays.items()}
    nc = bacc.Bacc("TRN2", target_bir_lowering=False, num_devices=1, dynamic_dma_scratch_size=1024)
    aps = [nc.dram_tensor(k, a.shape, F32, kind="ExternalInput").ap() for k, a in arrays.items()]
    out = nc.dram_tensor("outT", (P, KT, SEQ), F32, kind="ExternalOutput").ap()
    trunk(nc, *aps, out)
    r = run_bass_kernel_spmd(nc, [arrays], core_ids=[0])
    got = r.results[0]["outT"]
    return np.ascontiguousarray(got.transpose(2, 1, 0)).reshape(1, SEQ, D)
```
